# Optimizing a Trainium2 kernel written in Bass

```python
import math
import jax, jax.numpy as jnp
from jax import lax
import numpy as np

D_MODEL = 1024
BATCH = 1
SEQ = 256
DEPTH = 1

HEAD_DIM = 64
D_MIX = D_MODEL
MOBA_HEADS = 8
MOBA_BLOCK = 256
MOBA_TOPK = 3
DIFF_HEADS = 4
DIFF_V_DIM = 2 * HEAD_DIM
Q_BLOCK = 128
MOBA_W = MOBA_HEADS * HEAD_DIM
DIFF_QK_W = DIFF_HEADS * 2 * HEAD_DIM
DIFF_V_W = DIFF_HEADS * DIFF_V_DIM
PROJ_COLS = 3 * MOBA_W + 2 * DIFF_QK_W + DIFF_V_W
SPLITS = (MOBA_W, 2 * MOBA_W, 3 * MOBA_W, 3 * MOBA_W + DIFF_QK_W, 3 * MOBA_W + 2 * DIFF_QK_W)
PEER_HEADS = 8
PEER_N_KEYS = 128
PEER_N_EXPERTS = PEER_N_KEYS * PEER_N_KEYS
PEER_D_QUERY = 256
PEER_D_HALF = PEER_D_QUERY // 2
PEER_TOPK = 16
PEER_CHUNK = 128
RMS_EPS = 1e-6

kernel_name = 'hybrid_moba_diffattn_peer_layer'

def rms_norm(x, g):
    xf = x.astype(jnp.float32)
    y = xf * lax.rsqrt(jnp.mean(xf * xf, axis=-1, keepdims=True) + RMS_EPS)
    return (y * g.astype(jnp.float32)).astype(x.dtype)

def alibi_slopes(n):
    return jnp.asarray(2.0 ** (-8.0 * np.arange(1, n + 1) / n), dtype=jnp.float32)

def lambda_init_fn(layer):
    return 0.8 - 0.6 * math.exp(-0.3 * layer)

def split_heads(t, n, dh):
    b, s, _ = t.shape
    return t.reshape(b, s, n, dh).transpose(0, 2, 1, 3)

def moba_query_block(q_blk, idx, k_blocks, v_blocks, q_start, slopes):
    n_h, n_q, d = q_blk.shape
    kk = idx.shape[-1]
    scale = d ** -0.5
    pos_q = q_start + jnp.arange(n_q, dtype=jnp.int32)
    own = q_start // MOBA_BLOCK
    blk_off = jnp.arange(MOBA_BLOCK, dtype=jnp.int32)
    h_ix = jnp.arange(n_h)[:, None, None]
    k_sel = k_blocks[h_ix, idx]
    v_sel = v_blocks[h_ix, idx]
    pos_sel = idx[..., None] * MOBA_BLOCK + blk_off
    s_sel = jnp.einsum('hqd,hqkjd->hqkj', q_blk, k_sel).astype(jnp.float32) * scale
    s_sel = s_sel - slopes[:, None, None, None] * (pos_q[None, :, None, None] - pos_sel).astype(jnp.float32)
    s_sel = jnp.where((idx < own)[..., None], s_sel, -jnp.inf)
    k_own = lax.dynamic_index_in_dim(k_blocks, own, axis=1, keepdims=False)
    v_own = lax.dynamic_index_in_dim(v_blocks, own, axis=1, keepdims=False)
    dist_own = pos_q[:, None] - (own * MOBA_BLOCK + blk_off)[None, :]
    s_own = jnp.einsum('hqd,hjd->hqj', q_blk, k_own).astype(jnp.float32) * scale
    s_own = s_own - slopes[:, None, None] * dist_own.astype(jnp.float32)
    s_own = jnp.where(dist_own >= 0, s_own, -jnp.inf)
    s = jnp.concatenate([s_sel.reshape(n_h, n_q, kk * MOBA_BLOCK), s_own], axis=-1)
    p = jax.nn.softmax(s, axis=-1).astype(v_own.dtype)
    p_sel = p[..., :kk * MOBA_BLOCK].reshape(n_h, n_q, kk, MOBA_BLOCK)
    p_own = p[..., kk * MOBA_BLOCK:]
    return jnp.einsum('hqkj,hqkjd->hqd', p_sel, v_sel) + jnp.einsum('hqj,hjd->hqd', p_own, v_own)

def moba_attention(q, k, v):
    b, n_h, s, d = q.shape
    nb = -(-s // MOBA_BLOCK)
    kk = min(MOBA_TOPK, nb)
    pad = nb * MOBA_BLOCK - s
    k_blocks = jnp.pad(k, ((0, 0), (0, 0), (0, pad), (0, 0))).reshape(b, n_h, nb, MOBA_BLOCK, d)
    v_blocks = jnp.pad(v, ((0, 0), (0, 0), (0, pad), (0, 0))).reshape(b, n_h, nb, MOBA_BLOCK, d)
    k_mean = jnp.mean(k_blocks.astype(jnp.float32), axis=3)
    gate = jnp.einsum('bhsd,bhnd->bhsn', q.astype(jnp.float32), k_mean)
    pos = jnp.arange(s, dtype=jnp.int32)
    past = jnp.arange(nb, dtype=jnp.int32)[None, :] < (pos // MOBA_BLOCK)[:, None]
    gate = jnp.where(past, gate, -jnp.inf)
    _, sel = lax.top_k(gate, kk)
    nqb = s // Q_BLOCK
    q_r = q.reshape(b, n_h, nqb, Q_BLOCK, d).transpose(0, 2, 1, 3, 4)
    sel_r = sel.reshape(b, n_h, nqb, Q_BLOCK, kk).transpose(0, 2, 1, 3, 4)
    starts = jnp.arange(nqb, dtype=jnp.int32) * Q_BLOCK
    slopes = alibi_slopes(n_h)

    def per_batch(args):
        q_b, sel_b, kb, vb = args
        return lax.map(lambda a: moba_query_block(a[0], a[1], kb, vb, a[2], slopes), (q_b, sel_b, starts))

    out = lax.map(per_batch, (q_r, sel_r, k_blocks, v_blocks))
    return out.transpose(0, 1, 3, 2, 4).reshape(b, s, n_h * d)

def diff_attention(q1, q2, k1, k2, v, lam):
    b, n_h, s, d = q1.shape
    scale = d ** -0.5
    slopes = alibi_slopes(n_h)[:, None, None]
    outs = []
    for i in range(s // Q_BLOCK):
        s0, e = i * Q_BLOCK, (i + 1) * Q_BLOCK
        dist = (jnp.arange(s0, e)[:, None] - jnp.arange(e)[None, :]).astype(jnp.float32)
        bias = jnp.where(dist >= 0, -slopes * dist, -jnp.inf)
        a1 = jax.nn.softmax(jnp.einsum('bhqd,bhkd->bhqk', q1[:, :, s0:e], k1[:, :, :e]).astype(jnp.float32) * scale + bias, axis=-1)
        a2 = jax.nn.softmax(jnp.einsum('bhqd,bhkd->bhqk', q2[:, :, s0:e], k2[:, :, :e]).astype(jnp.float32) * scale + bias, axis=-1)
        a = (a1 - lam * a2).astype(v.dtype)
        outs.append(jnp.einsum('bhqk,bhkd->bhqd', a, v[:, :, :e]))
    return jnp.concatenate(outs, axis=2)

def peer_ffn(x, w_query, sub_keys, u, v):
    b, s, dm = x.shape
    xt = x.reshape(b * s // PEER_CHUNK, PEER_CHUNK, dm)

    def chunk(xc):
        q = (xc @ w_query).reshape(PEER_CHUNK, PEER_HEADS, 2, PEER_D_HALF)
        sc = jnp.einsum('chpd,hpnd->chpn', q, sub_keys).astype(jnp.float32)
        s1, i1 = lax.top_k(sc[:, :, 0], PEER_TOPK)
        s2, i2 = lax.top_k(sc[:, :, 1], PEER_TOPK)
        cand = (s1[..., :, None] + s2[..., None, :]).reshape(PEER_CHUNK, PEER_HEADS, PEER_TOPK * PEER_TOPK)
        cand_idx = (i1[..., :, None] * PEER_N_KEYS + i2[..., None, :]).reshape(PEER_CHUNK, PEER_HEADS, PEER_TOPK * PEER_TOPK)
        best, pos = lax.top_k(cand, PEER_TOPK)
        experts = jnp.take_along_axis(cand_idx, pos, axis=-1)
        g = jax.nn.softmax(best, axis=-1)
        u_sel = u[experts]
        v_sel = v[experts]
        h = jax.nn.gelu(jnp.einsum('cd,chkd->chk', xc, u_sel), approximate=False)
        act = (h.astype(jnp.float32) * g).astype(v_sel.dtype)
        return jnp.einsum('chk,chkd->cd', act, v_sel)

    return lax.map(chunk, xt).reshape(b, s, dm)

def setup_inputs(seed: int = 0) -> dict:
    key = jax.random.key(seed)
    ks = jax.random.split(key, 13)
    f32 = jnp.float32

    def nrm(k, shape, scale):
        return jax.random.normal(k, shape, f32) * scale

    def gain(k, shape):
        return 1.0 + 0.02 * jax.random.normal(k, shape, f32)

    return {
        'x': nrm(ks[0], (BATCH, SEQ, D_MODEL), 1.0),
        'norm1_g': gain(ks[1], (DEPTH, D_MODEL)),
        'w_in': nrm(ks[2], (DEPTH, D_MODEL, PROJ_COLS), D_MODEL ** -0.5),
        'moba_qk_norm_g': gain(ks[3], (DEPTH, 2, HEAD_DIM)),
        'diff_qk_norm_g': gain(ks[4], (DEPTH, 2, HEAD_DIM)),
        'diff_lambda': nrm(ks[5], (DEPTH, 4, HEAD_DIM), 0.1),
        'diff_subln_g': gain(ks[6], (DEPTH, DIFF_V_DIM)),
        'w_out': nrm(ks[7], (DEPTH, D_MIX, D_MODEL), D_MIX ** -0.5),
        'norm2_g': gain(ks[8], (DEPTH, D_MODEL)),
        'peer_w_query': nrm(ks[9], (DEPTH, D_MODEL, PEER_HEADS * PEER_D_QUERY), D_MODEL ** -0.5),
        'peer_sub_keys': nrm(ks[10], (DEPTH, PEER_HEADS, 2, PEER_N_KEYS, PEER_D_HALF), PEER_D_HALF ** -0.5),
        'peer_u': nrm(ks[11], (DEPTH, PEER_N_EXPERTS, D_MODEL), D_MODEL ** -0.5),
        'peer_v': nrm(ks[12], (DEPTH, PEER_N_EXPERTS, D_MODEL), 0.3),
    }

def reference(x, norm1_g, w_in, moba_qk_norm_g, diff_qk_norm_g, diff_lambda, diff_subln_g, w_out, norm2_g, peer_w_query, peer_sub_keys, peer_u, peer_v):
    b, s, _ = x.shape
    for l in range(DEPTH):
        lam_init = lambda_init_fn(l)
        h = rms_norm(x, norm1_g[l])
        proj = h @ w_in[l]
        mq, mk, mv, dq, dk, dv = jnp.split(proj, SPLITS, axis=-1)
        mq = rms_norm(split_heads(mq, MOBA_HEADS, HEAD_DIM), moba_qk_norm_g[l, 0])
        mk = rms_norm(split_heads(mk, MOBA_HEADS, HEAD_DIM), moba_qk_norm_g[l, 1])
        moba_out = moba_attention(mq, mk, split_heads(mv, MOBA_HEADS, HEAD_DIM))
        dq = rms_norm(dq.reshape(b, s, DIFF_HEADS, 2, HEAD_DIM).transpose(0, 2, 3, 1, 4), diff_qk_norm_g[l, 0])
        dk = rms_norm(dk.reshape(b, s, DIFF_HEADS, 2, HEAD_DIM).transpose(0, 2, 3, 1, 4), diff_qk_norm_g[l, 1])
        lam_p = diff_lambda[l].astype(jnp.float32)
        lam = jnp.exp(jnp.dot(lam_p[0], lam_p[1])) - jnp.exp(jnp.dot(lam_p[2], lam_p[3])) + lam_init
        diff_o = diff_attention(dq[:, :, 0], dq[:, :, 1], dk[:, :, 0], dk[:, :, 1], split_heads(dv, DIFF_HEADS, DIFF_V_DIM), lam)
        diff_o = rms_norm(diff_o, diff_subln_g[l]) * (1.0 - lam_init)
        diff_out = diff_o.transpose(0, 2, 1, 3).reshape(b, s, DIFF_V_W)
        x = x + jnp.concatenate([moba_out, diff_out], axis=-1) @ w_out[l]
        x = x + peer_ffn(rms_norm(x, norm2_g[l]), peer_w_query[l], peer_sub_keys[l], peer_u[l], peer_v[l])
    return x


_drawn_inputs = setup_inputs


def setup_inputs(seed=0):
    import zlib

    import numpy as np

    out = dict(_drawn_inputs(seed))
    spreads = {}
    factors = {'moba_qk_norm_g': 5.768, 'diff_qk_norm_g': 3.136, 'diff_subln_g': 3.366, 'norm2_g': 3.195}
    for name, (base, spread) in spreads.items():
        noise = np.random.default_rng([zlib.crc32(name.encode()), seed]).standard_normal(out[name].shape)
        drawn = base * np.exp(spread * noise) if base else spread * noise
        out[name] = __import__('jax').numpy.asarray(drawn.astype(out[name].dtype))
    for name, factor in factors.items():
        out[name] = (out[name] * factor).astype(out[name].dtype)
    return out
```

```python
import math
from contextlib import ExitStack

import concourse.bass as bass
from concourse import mybir

F32 = mybir.dt.float32
F32R = mybir.dt.float32r
U32 = mybir.dt.uint32
ALU = mybir.AluOpType
ACT = mybir.ActivationFunctionType
AX = mybir.AxisListType

P = 128
SEQ = 256
D = 1024
HALVES = SEQ // P
KD = D // P
HEAD = 64
MOBA_HEADS = 8
DIFF_HEADS = 4
COLS = 512
TOPK = 16
PEER_HEADS = 8
N_KEYS = 128
SLOTS = PEER_HEADS * TOPK
HP = PEER_HEADS * 2
TILES = N_KEYS
EPS = 1e-6
LAM_INIT = 0.8 - 0.6 * math.exp(-0.3 * 0)
MASKED = -1.0e30
REMOVED = -3.0e38
W_SLOTS = 4
LAG = 8
BLOCK_ORDER = [0, 1, 3, 4, 2, 5]
QK_GROUPS = 4 * HALVES
GROUPS = 6 * HALVES
MOBA_N = MOBA_HEADS
INSTANCES = MOBA_HEADS + 2 * DIFF_HEADS
MIXES = MOBA_HEADS + DIFF_HEADS
TOK_STEP = 8
G1, G2, GQK, GSUB = 0, 8, 16, 20
N_GAINS = 21


def layer(nc, x, norm1_g, w_in, moba_g, diff_g, diff_lambda, subln_g, w_out, norm2_g, w_query, sub_keys,
          peer_u, peer_v, out):
    keep = ExitStack()

    base = (nc.sbuf_base + 31) // 32 * 32

    class Region:
        def __init__(self, at):
            self.at = at

        def put(self, name, shape, dt=F32):
            t = nc.alloc_sbuf_tensor_at(name, shape, dt, offset=self.at)
            size = 4
            for n in shape[1:]:
                size *= n
            self.at += (size + 31) // 32 * 32
            return t

    whole = Region(base)
    ident = whole.put("ident", [P, P])
    gains = whole.put("gains", [P, N_GAINS])
    routes = whole.put("routes", [P, 3, SEQ])
    xn_hi = whole.put("xn_hi", [P, KD, SEQ], F32R)
    xn_lo = whole.put("xn_lo", [P, KD, SEQ], F32R)
    stream_at = whole.at
    u_raw = whole.put("u_raw", [P, 2, D])
    v_raw = whole.put("v_raw", [P, 2, D])
    ut_hi = whole.put("ut_hi", [P, 2, KD, P], F32R)
    ut_lo = whole.put("ut_lo", [P, 2, KD, P], F32R)
    h_ring = whole.put("h_ring", [P, LAG, SEQ])
    act_hi = whole.put("act_hi", [P, 2, SEQ], F32R)
    act_lo = whole.put("act_lo", [P, 2, SEQ], F32R)
    split_at = whole.at
    v_hi = whole.put("v_hi", [P, 2, D], F32R)
    v_lo = whole.put("v_lo", [P, 2, D], F32R)
    arena_at = whole.at
    gate_m = whole.put("gate_m", [P, SEQ, N_KEYS])

    over = Region(split_at)
    hot1 = over.put("hot1", [P, TOK_STEP, N_KEYS])
    hot2 = over.put("hot2", [P, TOK_STEP, N_KEYS])
    iota_row = over.put("iota_row", [P, P])

    over = Region(arena_at)
    w_ring = over.put("w_ring", [P, W_SLOTS, KD, COLS])
    featT = over.put("featT", [P, KD, SEQ])
    skT = over.put("skT", [P, HP, N_KEYS])
    routing_at = over.at
    bias_t = over.put("bias_t", [P, MOBA_HEADS, 3 * P])
    v_sb = over.put("v_sb", [P, 2, HALVES, COLS])
    x_sb = over.put("x_sb", [P, HALVES, D])
    scaled = over.put("scaled", [P, HALVES, D])
    gain_rows = over.put("gain_rows", [N_GAINS, P])
    lam_in = over.put("lam_in", [P, 4 * HEAD])
    lam_prod = over.put("lam_prod", [P, 2, HEAD])
    tiny = {}
    for name, n in (("ssq", 2), ("ms", 2), ("sd", 2), ("rstd", 2), ("dots", 2), ("edots", 2), ("lam", 2),
                    ("qk_ss", 64), ("qk_ms", 64), ("qk_sd", 64), ("qk_rs", 64), ("nmax", 32), ("sums", 32),
                    ("rsum", 32), ("rlam", 8), ("d_ss", 8), ("d_ms", 8), ("d_sd", 8), ("d_rs", 8),
                    ("ssq2", 4), ("ms2", 2), ("sd2", 2), ("rstd2", 2), ("ssq2s", 2)):
        tiny[name] = over.put("t_" + name, [P, n])
    assert over.at <= arena_at + 4 * SEQ * N_KEYS

    over = Region(stream_at)
    qkT = over.put("qkT", [P, 4, 4, SEQ])
    sk_nat = over.put("sk_nat", [P, HP, P])
    normed = over.put("normed", [P, 2, COLS])
    squares = over.put("squares", [P, 2, COLS])
    logits = over.put("logits", [P, 2, 3 * P])
    expd = over.put("expd", [P, 4, 3 * P])
    mixed = over.put("mixed", [P, 2, 3 * P])
    probsT = over.put("probsT", [P, 2, 3 * P])
    assert over.at <= split_at + 16384 - 512
    over = Region(stream_at)
    qT = over.put("qT", [P, 2, SEQ])
    over = Region(routing_at)
    scores = over.put("scores", [P, HALVES, HP, N_KEYS])
    key_val = over.put("key_val", [P, HP, TOPK])
    key_idx = over.put("key_idx", [P, HP, TOPK], U32)
    key_idf = over.put("key_idf", [P, HP, TOPK])
    cand = over.put("cand", [P, PEER_HEADS, TOPK, TOPK])
    match = over.put("match", [P, PEER_HEADS, TOPK, TOPK])
    best = over.put("best", [P, PEER_HEADS, TOPK])
    pos = over.put("pos", [P, PEER_HEADS, TOPK], U32)
    pos_u = over.put("pos_u", [P, 2, SLOTS], U32)
    pos_f = over.put("pos_f", [P, 2, SLOTS])
    chosen = over.put("chosen", [P, 3, SLOTS])
    gsum = over.put("gsum", [P, 2, PEER_HEADS])
    assert over.at <= arena_at + 4 * SEQ * N_KEYS

    with keep:
        ps = [keep.enter_context(nc.psum_tensor(f"bank{i}", [P, COLS], F32)) for i in range(8)]

        def sem(name):
            return keep.enter_context(nc.semaphore(name))

        x_loaded = [sem(f"x_loaded{h}") for h in range(HALVES)]
        gains_loaded = sem("gains_loaded")
        lam_loaded = sem("lam_loaded")
        sk_loaded = sem("sk_loaded")
        w_loaded = [sem(f"w_loaded{i}") for i in range(W_SLOTS)]
        u_loaded = [sem(f"u_loaded{i}") for i in range(2)]
        v_loaded = [sem(f"v_loaded{i}") for i in range(2)]
        stored = sem("stored")
        ident_ready = sem("ident_ready")
        pool_step = sem("pool_step")
        bias_ready = sem("bias_ready")
        iota_ready = sem("iota_ready")
        dve_step = sem("dve_step")
        gainsT_done = sem("gainsT_done")
        gains_ready = sem("gains_ready")
        ssq_done = sem("ssq_done")
        ms_ready = sem("ms_ready")
        sd_ready = sem("sd_ready")
        scaled_ready = sem("scaled_ready")
        feat_done = sem("feat_done")
        feat_ready = sem("feat_ready")
        proj_done = sem("proj_done")
        w_used = sem("w_used")
        sq_done = sem("sq_done")
        qk_ms_ready = sem("qk_ms_ready")
        qk_sd_ready = sem("qk_sd_ready")
        normed_ready = sem("normed_ready")
        qkT_done = sem("qkT_done")
        qkT_ready = sem("qkT_ready")
        values_ready = sem("values_ready")
        skT_done = sem("skT_done")
        skT_ready = sem("skT_ready")
        logits_done = sem("logits_done")
        nmax_ready = sem("nmax_ready")
        exp_done = sem("exp_done")
        mixed_ready = sem("mixed_ready")
        probsT_done = sem("probsT_done")
        probsT_ready = sem("probsT_ready")
        heads_done = sem("heads_done")
        dots_ready = sem("dots_ready")
        edots_ready = sem("edots_ready")
        d_sq_done = sem("d_sq_done")
        d_ms_ready = sem("d_ms_ready")
        d_sd_ready = sem("d_sd_ready")
        mix_ready = sem("mix_ready")
        x2_done = sem("x2_done")
        xn_full = sem("xn_full")
        xn_hi_done = sem("xn_hi_done")
        xn_lo_done = sem("xn_lo_done")
        query_done = sem("query_done")
        query_ready = sem("query_ready")
        scores_done = sem("scores_done")
        scores_ready = sem("scores_ready")
        chosen_ready = sem("chosen_ready")
        routesT_done = sem("routesT_done")
        routes_ready = sem("routes_ready")
        hot_ready = sem("hot_ready")
        gate_done = sem("gate_done")
        gate_ready = sem("gate_ready")
        ut_done = sem("ut_done")
        ut_hi_done = sem("ut_hi_done")
        ut_lo_done = sem("ut_lo_done")
        h_done = sem("h_done")
        gelu_done = sem("gelu_done")
        act_done = sem("act_done")
        act_hi_done = sem("act_hi_done")
        act_lo_done = sem("act_lo_done")
        v_hi_done = sem("v_hi_done")
        v_lo_done = sem("v_lo_done")
        v_used = sem("v_used")
        y_ready = sem("y_ready")

        def need(eng, s, value):
            if not isinstance(value, int) or value > 0:
                eng.wait_ge(s, value)

        def w_source(w):
            if w < 6:
                m, c = w_in, BLOCK_ORDER[w]
            elif w < 8:
                m, c = w_out, w - 6
            else:
                m, c = w_query, w - 8
            return m[0, :, c * COLS:(c + 1) * COLS].rearrange("(k p) n -> p k n", p=P)

        def instance(n):
            if n < MOBA_HEADS:
                return 0, 1, n // 2, HEAD * (n % 2), n
            i, j = divmod(n - MOBA_HEADS, 2)
            return 2, 3, i, HEAD * j, 2 * i + 1

        def exps_for(m):
            return m + 1 if m < MOBA_HEADS else MOBA_HEADS + 2 * (m - MOBA_HEADS) + 2

        block = keep.enter_context(nc.Block())

        @block.sync
        def _(sp):
            for h in range(HALVES):
                sp.dma_start(x_sb[:, h, :], x[0, h * P:(h + 1) * P, :]).then_inc(x_loaded[h], 16)
            sp.dma_start(w_ring[:, 0, :, :], w_source(0)).then_inc(w_loaded[0], 16)
            rows = [(G1, KD, norm1_g[0].rearrange("(r c) -> r c", c=P)), (G2, KD, norm2_g[0].rearrange("(r c) -> r c", c=P)),
                    (GSUB, 1, subln_g)]
            for r, n, src in rows:
                sp.dma_start(gain_rows[r:r + n, :], src).then_inc(gains_loaded, 16)
            for r, src in ((GQK, moba_g[0]), (GQK + 2, diff_g[0])):
                for c in range(2):
                    sp.dma_start(gain_rows[r:r + 2, c * HEAD:(c + 1) * HEAD], src).then_inc(gains_loaded, 16)
            sp.dma_start(lam_in[:, :], diff_lambda.rearrange("a b c -> a (b c)").to_broadcast([P, 4 * HEAD]))\
              .then_inc(lam_loaded, 16)
            for w in range(1, 12):
                if w >= W_SLOTS:
                    sp.wait_ge(w_used, w - W_SLOTS + 1)
                sp.dma_start(w_ring[:, w % W_SLOTS, :, :], w_source(w)).then_inc(w_loaded[w % W_SLOTS], 16)
                if w == 3:
                    sp.dma_start(sk_nat[:, :, :], sub_keys[0].rearrange("h a n d -> n (h a) d")).then_inc(sk_loaded, 16)

            def load_u(t, p, held=True):
                if held:
                    sp.wait_ge(ut_done, 2 * t - 2)
                sp.dma_start(u_raw[:, p, :], peer_u[0, bass.ds(t * P, P), :]).then_inc(u_loaded[p], 16)

            def load_v(t, p, held=True):
                if held:
                    sp.wait_ge(v_lo_done, t - 1)
                sp.dma_start(v_raw[:, p, :], peer_v[0, bass.ds(t * P, P), :]).then_inc(v_loaded[p], 16)

            sp.wait_ge(scores_done, HP)
            for t in range(2):
                load_u(t, t, False)
            with sp.Fori(0, (LAG - 2) // 2) as turn:
                t = turn * 2 + 2
                for p in range(2):
                    load_u(t + p, p)
            for p in range(2):
                load_v(p, p, False)
                load_u(LAG + p, p)
            with sp.Fori(0, (TILES - (LAG + 2)) // 2) as turn:
                t = turn * 2 + (LAG + 2)
                for p in range(2):
                    load_u(t + p, p)
                    load_v(t + (p - LAG), p)
            with sp.Fori(0, LAG // 2) as turn:
                t = turn * 2 + (TILES - LAG)
                for p in range(2):
                    load_v(t + p, p)
            sp.wait_ge(y_ready, 4)
            for h in range(HALVES):
                sp.dma_start(out[0, h * P:(h + 1) * P, :], gate_m[:, 8 * h:8 * h + 8, :].rearrange("p a b -> p (a b)"))\
                  .then_inc(stored, 16)
            sp.wait_ge(stored, 16 * HALVES)

        @block.gpsimd
        def _(pool):
            pool.memset(ident[:, :], 0.0).then_inc(pool_step, 1)
            pool.wait_ge(pool_step, 1)
            pool.affine_select(out=ident[:, :], in_=ident[:, :], compare_op=ALU.not_equal, fill=1.0, base=0,
                               pattern=[[-1, P]], channel_multiplier=1).then_inc(ident_ready, 1)
            pool.iota(iota_row[:, :], pattern=[[1, P]], base=0, channel_multiplier=0,
                      allow_small_or_imprecise_dtypes=True).then_inc(iota_ready, 1)
            dist = bias_t[:, 0, :]
            pool.iota(dist[:, 0:P], pattern=[[1, P]], base=0, channel_multiplier=-1,
                      allow_small_or_imprecise_dtypes=True).then_inc(pool_step, 1)
            pool.iota(dist[:, P:3 * P], pattern=[[1, 2 * P]], base=-P, channel_multiplier=-1,
                      allow_small_or_imprecise_dtypes=True).then_inc(pool_step, 1)
            pool.wait_ge(pool_step, 3)
            for h in range(MOBA_HEADS - 1, -1, -1):
                if h == 0:
                    pool.wait_ge(pool_step, 3 + MOBA_HEADS - 1)
                pool.tensor_scalar(bias_t[:, h, :], dist[:, :], 2.0 ** -(h + 1), None, ALU.mult).then_inc(pool_step, 1)
            pool.wait_ge(pool_step, 3 + MOBA_HEADS)
            pool.affine_select(out=bias_t[:, :, 0:P], in_=bias_t[:, :, 0:P], compare_op=ALU.is_ge, fill=MASKED,
                               base=0, pattern=[[0, MOBA_HEADS], [-1, P]], channel_multiplier=1)\
                .then_inc(bias_ready, 1)
            pool.affine_select(out=bias_t[:, :, P:3 * P], in_=bias_t[:, :, P:3 * P], compare_op=ALU.is_ge, fill=MASKED,
                               base=P, pattern=[[0, MOBA_HEADS], [-1, 2 * P]], channel_multiplier=1)\
                .then_inc(bias_ready, 1)

        @block.scalar
        def _(act):
            for h in range(HALVES):
                act.wait_ge(x_loaded[h], 16)
                act.activation(scaled[:, h, :], x_sb[:, h, :], ACT.Square, accum_out=tiny["ssq"][:, h:h + 1])\
                   .then_inc(ssq_done, 1)
            act.wait_ge(gainsT_done, 1)
            act.activation(gains[:, :], ps[5][:, 0:N_GAINS], ACT.Copy).then_inc(gains_ready, 1)
            act.wait_ge(ms_ready, 1)
            act.activation(tiny["sd"][:, :], tiny["ms"][:, :], ACT.Sqrt).then_inc(sd_ready, 1)
            act.wait_ge(gains_ready, 1)
            act.activation(gains[:, GQK:GQK + 3:2], gains[:, GQK:GQK + 3:2], ACT.Copy, scale=HEAD ** -0.5)\
               .then_inc(gains_ready, 1)
            act.activation(gains[:, GSUB:GSUB + 1], gains[:, GSUB:GSUB + 1], ACT.Copy, scale=1.0 - LAM_INIT)\
               .then_inc(gains_ready, 1)
            act.wait_ge(gains_ready, 3)

            def feat_evac(rnd, pair, bank, gain):
                act.wait_ge(feat_done, rnd * 4 + pair + 1)
                for i in range(2):
                    k = 2 * pair + i
                    ins = act.activation(featT[:, k, :], ps[bank][:, i * SEQ:(i + 1) * SEQ], ACT.Copy,
                                         scale=1.0 if gain(k) is None else gain(k))
                ins.then_inc(feat_ready, 1)

            for pair in range(4):
                feat_evac(0, pair, 6 + pair % 2, lambda k: gains[:, G1 + k:G1 + k + 1])

            def qkT_evac(g):
                b, h = divmod(g, HALVES)
                act.wait_ge(qkT_done, g + 1)
                act.activation(qkT[:, b, :, h * P:(h + 1) * P], ps[4 + g % 2][:, :].rearrange("p (b t) -> p b t", b=4),
                               ACT.Copy, scale=gains[:, GQK + b:GQK + b + 1]).then_inc(qkT_ready, 1)

            for g in range(GROUPS):
                if g < QK_GROUPS:
                    act.wait_ge(proj_done, g + 1)
                    if g >= 2:
                        act.wait_ge(qk_ms_ready, g - 1)
                    act.activation(squares[:, g % 2, :], ps[g % 4][:, :], ACT.Square).then_inc(sq_done, 1)
                    act.wait_ge(qk_ms_ready, g + 1)
                    act.activation(tiny["qk_sd"][:, 8 * g:8 * g + 8], tiny["qk_ms"][:, 8 * g:8 * g + 8], ACT.Sqrt)\
                       .then_inc(qk_sd_ready, 1)
                if 1 <= g <= QK_GROUPS:
                    qkT_evac(g - 1)
                if g >= QK_GROUPS:
                    i, h = divmod(g - QK_GROUPS, HALVES)
                    act.wait_ge(proj_done, g + 1)
                    act.activation(v_sb[:, i, h, :], ps[g % 4][:, :], ACT.Copy).then_inc(values_ready, 1)
            for j in range(4):
                act.wait_ge(skT_done, j + 1)
                act.activation(skT[:, 4 * j:4 * j + 4, :], ps[4 + j % 2][:, :].rearrange("p (a n) -> p a n", a=4), ACT.Copy)\
                   .then_inc(skT_ready, 1)
            act.wait_ge(dots_ready, 2)
            act.activation(tiny["edots"][:, :], tiny["dots"][:, :], ACT.Exp).then_inc(edots_ready, 1)

            def exps(n):
                act.wait_ge(nmax_ready, n + 1)
                if n >= 4:
                    if n < 12:
                        act.wait_ge(probsT_done, n - 3)
                    else:
                        act.wait_ge(mixed_ready, (n - 12) // 2 + 1)
                for h, lo, hi in ((0, 0, P), (1, P, 3 * P)):
                    c = h * INSTANCES + n
                    ins = act.activation(expd[:, n % 4, lo:hi], logits[:, n % 2, lo:hi], ACT.Exp,
                                         bias=tiny["nmax"][:, c:c + 1], accum_out=tiny["sums"][:, c:c + 1])
                ins.then_inc(exp_done, 1)

            def probs_evac(m):
                act.wait_ge(probsT_done, m + 1)
                if m >= 2:
                    act.wait_ge(heads_done, m - 1)
                act.activation(probsT[:, m % 2, :], ps[2 + m % 2][:, 0:3 * P], ACT.Copy).then_inc(probsT_ready, 1)

            n = 0
            for m in range(MIXES):
                while n < min(exps_for(m) + 1, INSTANCES):
                    exps(n)
                    n += 1
                probs_evac(m)
            act.wait_ge(heads_done, MIXES)
            for h in range(HALVES):
                act.activation(squares[:, h, :], ps[6 + h][:, :], ACT.Square).then_inc(d_sq_done, 1)
            act.wait_ge(d_ms_ready, 1)
            act.activation(tiny["d_sd"][:, :], tiny["d_ms"][:, :], ACT.Sqrt).then_inc(d_sd_ready, 1)
            for pair in range(4):
                feat_evac(1, pair, pair % 2, lambda k: None if k < 4 else gains[:, GSUB:GSUB + 1])
            for h in range(HALVES):
                for c in range(2):
                    act.wait_ge(x2_done, c + 1)
                    act.activation(scaled[:, h, c * COLS:(c + 1) * COLS], ps[4 + 2 * h + c][:, :], ACT.Square,
                                   accum_out=tiny["ssq2"][:, 2 * h + c:2 * h + c + 1]).then_inc(ssq_done, 1)
            act.wait_ge(ms_ready, 2)
            act.activation(tiny["sd2"][:, :], tiny["ms2"][:, :], ACT.Sqrt).then_inc(sd_ready, 1)
            for pair in range(4):
                feat_evac(2, pair, pair % 2, lambda k: gains[:, G2 + k:G2 + k + 1])
                act.wait_ge(feat_ready, 8 + pair + 1)
                act.activation(xn_hi[:, 2 * pair:2 * pair + 2, :], featT[:, 2 * pair:2 * pair + 2, :], ACT.Copy)\
                   .then_inc(xn_hi_done, 1)

            def scores_evac(hp):
                act.wait_ge(scores_done, hp + 1)
                act.activation(scores[:, :, hp, :], ps[hp % 2][:, 0:SEQ].rearrange("p (h n) -> p h n", h=2), ACT.Copy)\
                   .then_inc(scores_ready, 1)

            for hp in range(HP):
                act.wait_ge(query_done, hp + 1)
                if hp >= 2:
                    act.wait_ge(scores_done, hp - 1)
                act.activation(qT[:, hp % 2, :], ps[2 + hp % 2][:, 0:SEQ], ACT.Copy).then_inc(query_ready, 1)
                if hp >= 1:
                    scores_evac(hp - 1)
            scores_evac(HP - 1)
            for h in range(HALVES):
                act.wait_ge(edots_ready, 2 * h + 2)
                act.activation(best[:, :, :], best[:, :, :], ACT.Exp).then_inc(edots_ready, 1)

            with act.Fori(0, SEQ // TOK_STEP) as i:
                for b in range(2):
                    act.wait_ge(gate_done, 2 * i + (b + 1))
                    act.activation(gate_m[:, bass.ds(i * TOK_STEP + 4 * b, 4), :].rearrange("p a b -> p (a b)"),
                                   ps[b][:, :], ACT.Copy).then_inc(gate_ready, 1)

            def ut_split(t, p):
                for b in range(2):
                    need(act, ut_done, 2 * t + (b + 1))
                    if b == 0:
                        need(act, h_done, t - 1)
                    act.activation(ut_hi[:, p, 4 * b:4 * b + 4, :].rearrange("p a b -> p (a b)"), ps[b][:, :], ACT.Copy)\
                       .then_inc(ut_hi_done, 1)

            def v_split(t, slot):
                p = slot % 2
                need(act, act_done, t + 1)
                need(act, v_used, t - 1)
                act.activation(act_hi[:, p, :], h_ring[:, slot, :], ACT.Copy).then_inc(act_hi_done, 1)
                need(act, v_loaded[p], (t - p) * 8 + 16)
                act.activation(v_hi[:, p, :], v_raw[:, p, :], ACT.Copy).then_inc(v_hi_done, 1)

            def gelu(t, slot):
                need(act, h_done, t + 1)
                need(act, act_lo_done, t - (LAG - 1))
                act.activation(h_ring[:, slot, :], ps[2 + slot % 2][:, 0:SEQ], ACT.Gelu).then_inc(gelu_done, 1)

            def act_step(s, j, splits_u=True, splits_v=True, gelus=True):
                if splits_u:
                    ut_split(s + 1, (j + 1) % 2)
                if splits_v:
                    v_split(s - (LAG - 1), (j + 1) % LAG)
                if gelus:
                    gelu(s, j % LAG)

            ut_split(0, 0)
            for s in range(2 * LAG):
                act_step(s, s, splits_v=s >= LAG - 1)
            with act.Fori(0, (TILES - LAG - (2 * LAG)) // LAG) as turn:
                s = turn * LAG + (2 * LAG)
                for j in range(LAG):
                    act_step(s + j, j)
            for s in range(TILES - LAG, TILES + LAG - 1):
                act_step(s, s, splits_u=s + 1 < TILES, gelus=s < TILES)
            act.wait_ge(v_used, TILES)
            for c in range(2):
                act.activation(gate_m[:, 4 * c:4 * c + 4, :].rearrange("p a b -> p (a b)"), ps[4 + c][:, :], ACT.Copy)\
                   .then_inc(y_ready, 1)

        @block.vector
        def _(dve):
            steps = [0]

            def mark(ins):
                steps[0] += 1
                ins.then_inc(dve_step, 1)
                return steps[0]

            def link(ins):
                dve.wait_ge(dve_step, mark(ins))

            dve.wait_ge(ssq_done, 2)
            dve.tensor_scalar(tiny["ms"][:, :], tiny["ssq"][:, :], 1.0 / D, EPS, ALU.mult, ALU.add).then_inc(ms_ready, 1)
            dve.wait_ge(sd_ready, 1)
            link(dve.reciprocal(tiny["rstd"][:, :], tiny["sd"][:, :]))
            for h in range(HALVES):
                dve.tensor_scalar(scaled[:, h, :], x_sb[:, h, :], tiny["rstd"][:, h:h + 1], None, ALU.mult)\
                   .then_inc(scaled_ready, 1)
            dve.wait_ge(lam_loaded, 16)
            for i in range(2):
                dve.tensor_tensor_reduce(out=lam_prod[:, i, :], in0=lam_in[:, 2 * i * HEAD:(2 * i + 1) * HEAD],
                                         in1=lam_in[:, (2 * i + 1) * HEAD:(2 * i + 2) * HEAD], scale=1.0, scalar=0.0,
                                         op0=ALU.mult, op1=ALU.add, accum_out=tiny["dots"][:, i:i + 1])\
                   .then_inc(dots_ready, 1)
            for g in range(QK_GROUPS):
                cols = slice(8 * g, 8 * g + 8)
                dve.wait_ge(sq_done, g + 1)
                link(dve.tensor_reduce(tiny["qk_ss"][:, cols], squares[:, g % 2, :].rearrange("p (h d) -> p h d", d=HEAD),
                                       AX.X, ALU.add))
                dve.tensor_scalar(tiny["qk_ms"][:, cols], tiny["qk_ss"][:, cols], 1.0 / HEAD, EPS, ALU.mult, ALU.add)\
                   .then_inc(qk_ms_ready, 1)
                dve.wait_ge(qk_sd_ready, g + 1)
                link(dve.reciprocal(tiny["qk_rs"][:, cols], tiny["qk_sd"][:, cols]))
                if g >= 2:
                    dve.wait_ge(qkT_done, g - 1)
                dve.tensor_tensor(normed[:, g % 2, :].rearrange("p (h d) -> p h d", d=HEAD),
                                  ps[g % 4][:, :].rearrange("p (h d) -> p h d", d=HEAD),
                                  tiny["qk_rs"][:, cols].unsqueeze(2).to_broadcast([P, 8, HEAD]), ALU.mult)\
                   .then_inc(normed_ready, 1)
            dve.wait_ge(edots_ready, 1)
            link(dve.tensor_tensor(tiny["lam"][:, 0:1], tiny["edots"][:, 0:1], tiny["edots"][:, 1:2], ALU.subtract))
            link(dve.tensor_scalar(tiny["lam"][:, 1:2], tiny["lam"][:, 0:1], LAM_INIT, None, ALU.add))
            dve.wait_ge(bias_ready, 2)

            def bias_and_max(n):
                table = instance(n)[4]
                dve.wait_ge(logits_done, n + 1)
                if n >= 2:
                    dve.wait_ge(exp_done, n - 1)
                link(dve.tensor_tensor(logits[:, n % 2, :], ps[n % 2][:, 0:3 * P], bias_t[:, table, :], ALU.add))
                for h, lo, hi in ((0, 0, P), (1, P, 3 * P)):
                    c = h * INSTANCES + n
                    ins = dve.tensor_reduce(tiny["nmax"][:, c:c + 1], logits[:, n % 2, lo:hi], AX.X, ALU.max, negate=True)
                ins.then_inc(nmax_ready, 1)

            def mix_diff(i):
                n = MOBA_HEADS + 2 * i
                dve.wait_ge(exp_done, n + 2)
                if i >= 2:
                    dve.wait_ge(probsT_done, MOBA_HEADS + i - 1)
                for h in range(HALVES):
                    c = h * INSTANCES + n
                    ins = dve.reciprocal(tiny["rsum"][:, c:c + 2], tiny["sums"][:, c:c + 2])
                    at = mark(ins)
                dve.wait_ge(dve_step, at)
                for h in range(HALVES):
                    c = h * INSTANCES + n
                    at = mark(dve.tensor_scalar(tiny["rlam"][:, 2 * i + h:2 * i + h + 1], tiny["rsum"][:, c + 1:c + 2],
                                                tiny["lam"][:, 1:2], None, ALU.mult))
                dve.wait_ge(dve_step, at)
                for h, lo, hi in ((0, 0, P), (1, P, 3 * P)):
                    at = mark(dve.tensor_scalar(expd[:, (n + 1) % 4, lo:hi], expd[:, (n + 1) % 4, lo:hi],
                                                tiny["rlam"][:, 2 * i + h:2 * i + h + 1], None, ALU.mult))
                dve.wait_ge(dve_step, at)
                for h, lo, hi in ((0, 0, P), (1, P, 3 * P)):
                    c = h * INSTANCES + n
                    ins = dve.scalar_tensor_tensor(mixed[:, i % 2, lo:hi], expd[:, n % 4, lo:hi], tiny["rsum"][:, c:c + 1],
                                                   expd[:, (n + 1) % 4, lo:hi], ALU.mult, ALU.subtract)
                ins.then_inc(mixed_ready, 1)

            n = 0
            for m in range(MIXES):
                while n < min(exps_for(m) + 2, INSTANCES):
                    bias_and_max(n)
                    n += 1
                if m >= MOBA_HEADS:
                    mix_diff(m - MOBA_HEADS)
            dve.wait_ge(heads_done, MOBA_HEADS)
            for h in range(HALVES):
                c = h * INSTANCES
                at = mark(dve.reciprocal(tiny["rsum"][:, c:c + MOBA_HEADS], tiny["sums"][:, c:c + MOBA_HEADS]))
            dve.wait_ge(dve_step, at)
            for h in range(HALVES):
                c = h * INSTANCES
                dve.tensor_tensor(scaled[:, h, 0:COLS].rearrange("p (h d) -> p h d", d=HEAD),
                                  ps[4 + h][:, :].rearrange("p (h d) -> p h d", d=HEAD),
                                  tiny["rsum"][:, c:c + MOBA_HEADS].unsqueeze(2).to_broadcast([P, MOBA_HEADS, HEAD]),
                                  ALU.mult).then_inc(mix_ready, 1)
            for h in range(HALVES):
                dve.wait_ge(d_sq_done, h + 1)
                at = mark(dve.tensor_reduce(tiny["d_ss"][:, 4 * h:4 * h + 4],
                                            squares[:, h, :].rearrange("p (h d) -> p h d", d=P), AX.X, ALU.add))
            dve.wait_ge(dve_step, at)
            dve.tensor_scalar(tiny["d_ms"][:, :], tiny["d_ss"][:, :], 1.0 / P, EPS, ALU.mult, ALU.add).then_inc(d_ms_ready, 1)
            dve.wait_ge(d_sd_ready, 1)
            link(dve.reciprocal(tiny["d_rs"][:, :], tiny["d_sd"][:, :]))
            for h in range(HALVES):
                dve.tensor_tensor(scaled[:, h, COLS:D].rearrange("p (h d) -> p h d", d=P),
                                  ps[6 + h][:, :].rearrange("p (h d) -> p h d", d=P),
                                  tiny["d_rs"][:, 4 * h:4 * h + 4].unsqueeze(2).to_broadcast([P, DIFF_HEADS, P]),
                                  ALU.mult).then_inc(mix_ready, 1)
            dve.wait_ge(ssq_done, 2 + 4)
            link(dve.tensor_reduce(tiny["ssq2s"][:, :], tiny["ssq2"][:, :].rearrange("p (h c) -> p h c", c=2), AX.X, ALU.add))
            dve.tensor_scalar(tiny["ms2"][:, :], tiny["ssq2s"][:, :], 1.0 / D, EPS, ALU.mult, ALU.add).then_inc(ms_ready, 1)
            dve.wait_ge(sd_ready, 2)
            link(dve.reciprocal(tiny["rstd2"][:, :], tiny["sd2"][:, :]))
            for h in range(HALVES):
                for c in range(2):
                    ins = dve.tensor_scalar(scaled[:, h, c * COLS:(c + 1) * COLS], ps[4 + 2 * h + c][:, :],
                                            tiny["rstd2"][:, h:h + 1], None, ALU.mult)
                    ins.then_inc(scaled_ready, 1)
            for pair in range(4):
                dve.wait_ge(xn_hi_done, pair + 1)
                dve.tensor_tensor(xn_lo[:, 2 * pair:2 * pair + 2, :], featT[:, 2 * pair:2 * pair + 2, :],
                                  xn_hi[:, 2 * pair:2 * pair + 2, :].bitcast(F32), ALU.subtract).then_inc(xn_lo_done, 1)

            dve.wait_ge(iota_ready, 1)
            for h in range(HALVES):
                if h:
                    dve.wait_ge(routesT_done, h)
                def top16(n, values, found, index):
                    for r in range(2):
                        marks = []
                        for i in range(n):
                            if r == 0 and n == HP:
                                dve.wait_ge(scores_ready, i + 1)
                            marks.append(mark(dve.max(found(i, r), values(i))))
                        for i in range(n):
                            dve.wait_ge(dve_step, marks[i])
                            marks[i] = mark(dve.max_index(index(i, r), found(i, r), values(i)))
                        if r == 0:
                            for i in range(n):
                                dve.wait_ge(dve_step, marks[i])
                                marks[i] = mark(dve.match_replace(values(i), found(i, r), values(i), REMOVED))
                            dve.wait_ge(dve_step, marks[-1])
                    dve.wait_ge(dve_step, marks[-1])

                top16(HP, lambda i: scores[:, h, i, :], lambda i, r: key_val[:, i, 8 * r:8 * r + 8],
                      lambda i, r: key_idx[:, i, 8 * r:8 * r + 8])
                link(dve.tensor_copy(key_idf[:, :, :], key_idx[:, :, :]))
                pairs = key_val[:, :, :].rearrange("p (h a) k -> p h a k", a=2)
                shape = [P, PEER_HEADS, TOPK, TOPK]
                link(dve.tensor_tensor(cand[:, :, :, :], pairs[:, :, 0, :].unsqueeze(3).to_broadcast(shape),
                                       pairs[:, :, 1, :].unsqueeze(2).to_broadcast(shape), ALU.add))
                top16(PEER_HEADS, lambda i: cand[:, i, :, :].rearrange("p a b -> p (a b)"),
                      lambda i, r: best[:, i, 8 * r:8 * r + 8], lambda i, r: pos[:, i, 8 * r:8 * r + 8])
                wide = [P, PEER_HEADS, TOPK]
                link(dve.tensor_copy(gsum[:, 0, :], best[:, :, 0]))
                dve.tensor_tensor(best[:, :, :], best[:, :, :], gsum[:, 0, :].unsqueeze(2).to_broadcast(wide), ALU.subtract)\
                   .then_inc(edots_ready, 1)
                flat = pos[:, :, :].rearrange("p h k -> p (h k)")
                mark(dve.tensor_scalar(pos_u[:, 0, :], flat, 4, None, ALU.logical_shift_right))
                link(dve.tensor_scalar(pos_u[:, 1, :], flat, TOPK - 1, None, ALU.bitwise_and))
                link(dve.tensor_copy(pos_f[:, :, :], pos_u[:, :, :]))
                idx = key_idf[:, :, :].rearrange("p (h a) k -> p h a k", a=2)
                m3 = match[:, :, :, :].rearrange("p h s k -> p (h s) k")
                for a in range(2):
                    link(dve.tensor_tensor(m3, pos_f[:, a, :].unsqueeze(2).to_broadcast([P, SLOTS, TOPK]),
                                           iota_row[:, 0:TOPK].unsqueeze(1).to_broadcast([P, SLOTS, TOPK]), ALU.is_equal))
                    link(dve.tensor_tensor(match[:, :, :, :], match[:, :, :, :],
                                           idx[:, :, a, :].unsqueeze(2).to_broadcast(shape), ALU.mult))
                    link(dve.tensor_reduce(chosen[:, a, :], m3, AX.X, ALU.add))
                dve.wait_ge(edots_ready, 2 * h + 3)
                link(dve.tensor_reduce(gsum[:, 0, :], best[:, :, :], AX.X, ALU.add))
                link(dve.reciprocal(gsum[:, 1, :], gsum[:, 0, :]))
                dve.tensor_tensor(chosen[:, 2, :].rearrange("p (h k) -> p h k", k=TOPK), best[:, :, :],
                                  gsum[:, 1, :].unsqueeze(2).to_broadcast(wide), ALU.mult).then_inc(chosen_ready, 1)
                dve.wait_ge(routesT_done, h + 1)
                dve.tensor_copy(routes[:, :, h * P:(h + 1) * P], ps[h][:, 0:3 * P].rearrange("p (a t) -> p a t", a=3))\
                   .then_inc(routes_ready, 1)
            dve.wait_ge(routes_ready, HALVES)

            def hot_rows(i, first):
                for b in range(2):
                    if not first:
                        dve.wait_ge(gate_done, 2 * i + (b - 1))
                    for j in range(4 * b, 4 * b + 4):
                        tok = i * TOK_STEP + j
                        dve.tensor_scalar(hot1[:, j, :], iota_row[:, :], routes[:, 0, bass.ds(tok, 1)],
                                          routes[:, 2, bass.ds(tok, 1)], ALU.is_equal, ALU.mult)
                        ins = dve.tensor_scalar(hot2[:, j, :], iota_row[:, :], routes[:, 1, bass.ds(tok, 1)], None, ALU.is_equal)
                    ins.then_inc(hot_ready, 1)

            hot_rows(0, True)
            with dve.Fori(1, SEQ // TOK_STEP) as i:
                hot_rows(i, False)

            def gated(t, slot):
                need(dve, gelu_done, t + 1)
                dve.tensor_tensor(h_ring[:, slot, :], h_ring[:, slot, :],
                                  gate_m[:, :, bass.ds(t, 1)].rearrange("p c a -> p (c a)"), ALU.mult).then_inc(act_done, 1)

            def ut_rest(t, p):
                for b in range(2):
                    need(dve, ut_hi_done, 2 * t + (b + 1))
                    if b == 0:
                        need(dve, h_done, t - 1)
                    dve.tensor_tensor(ut_lo[:, p, 4 * b:4 * b + 4, :].rearrange("p a b -> p (a b)"), ps[b][:, :],
                                      ut_hi[:, p, 4 * b:4 * b + 4, :].rearrange("p a b -> p (a b)").bitcast(F32),
                                      ALU.subtract).then_inc(ut_lo_done, 1)

            def v_rest(t, slot):
                p = slot % 2
                need(dve, act_hi_done, t + 1)
                need(dve, v_used, t - 1)
                dve.tensor_tensor(act_lo[:, p, :], h_ring[:, slot, :], act_hi[:, p, :].bitcast(F32), ALU.subtract)\
                   .then_inc(act_lo_done, 1)
                need(dve, v_hi_done, t + 1)
                dve.tensor_tensor(v_lo[:, p, :], v_raw[:, p, :], v_hi[:, p, :].bitcast(F32), ALU.subtract)\
                   .then_inc(v_lo_done, 1)

            def dve_step_of(s, j, splits_u=True, splits_v=True):
                if splits_v:
                    gated(s - (LAG - 1), (j + 1) % LAG)
                if splits_u:
                    ut_rest(s + 1, (j + 1) % 2)
                if splits_v:
                    v_rest(s - (LAG - 1), (j + 1) % LAG)

            dve.wait_ge(gate_ready, SEQ // 4)
            ut_rest(0, 0)
            for s in range(2 * LAG):
                dve_step_of(s, s, splits_v=s >= LAG - 1)
            with dve.Fori(0, (TILES - LAG - (2 * LAG)) // LAG) as turn:
                s = turn * LAG + (2 * LAG)
                for j in range(LAG):
                    dve_step_of(s + j, j)
            for s in range(TILES - LAG, TILES + LAG - 1):
                dve_step_of(s, s, splits_u=s + 1 < TILES)
            dve.wait_ge(v_used, TILES)
            for c in range(2):
                dve.tensor_copy(gate_m[:, 8 + 4 * c:12 + 4 * c, :].rearrange("p a b -> p (a b)"), ps[6 + c][:, :])\
                   .then_inc(y_ready, 1)

        @block.tensor
        def _(pe):
            mm = pe.matmul
            pe.wait_ge(ident_ready, 1)
            pe.wait_ge(gains_loaded, 16 * 7)
            pe.transpose(ps[5][:, 0:N_GAINS], gain_rows[:, :], ident[0:N_GAINS, 0:N_GAINS]).then_inc(gainsT_done, 1)

            def feat_transposes(rnd, first_bank, src_sem, base_count):
                for pair in range(4):
                    if pair >= 2:
                        pe.wait_ge(feat_ready, rnd * 4 + pair - 1)
                    for i in range(2):
                        k = 2 * pair + i
                        for h in range(HALVES):
                            ins = pe.transpose(ps[first_bank + pair % 2][:, i * SEQ + h * P:i * SEQ + (h + 1) * P],
                                               scaled[:, h, k * P:(k + 1) * P], ident[:, :])
                    ins.then_inc(feat_done, 1)

            pe.wait_ge(scaled_ready, 2)
            feat_transposes(0, 6, None, None)
            pe.wait_ge(feat_ready, 4)

            def qk_transposes(g):
                pe.wait_ge(normed_ready, g + 1)
                if g >= 2:
                    pe.wait_ge(qkT_ready, g - 1)
                for b in range(4):
                    ins = pe.transpose(ps[4 + g % 2][:, b * P:(b + 1) * P], normed[:, g % 2, b * P:(b + 1) * P], ident[:, :])
                ins.then_inc(qkT_done, 1)

            pe.wait_ge(gains_ready, 1)
            for g in range(GROUPS):
                w, h = divmod(g, HALVES)
                if h == 0:
                    pe.wait_ge(w_loaded[w % W_SLOTS], 16 * (w // W_SLOTS + 1))
                if 4 <= g < QK_GROUPS + 4:
                    pe.wait_ge(normed_ready, g - 3)
                for k in range(KD):
                    ins = mm(ps[g % 4][:, :], featT[:, k, h * P:(h + 1) * P], w_ring[:, w % W_SLOTS, k, :],
                             start=k == 0, stop=k == KD - 1)
                ins.then_inc(proj_done, 1)
                if h == 1:
                    pe.wait_ge(proj_done, g + 1)
                    pe.sem_inc(w_used, 1)
                if 1 <= g <= QK_GROUPS:
                    qk_transposes(g - 1)
            pe.wait_ge(sk_loaded, 16)
            for j in range(4):
                pe.wait_ge(qkT_ready, QK_GROUPS)
                if j >= 2:
                    pe.wait_ge(skT_ready, j - 1)
                for i in range(4):
                    ins = pe.transpose(ps[4 + j % 2][:, i * P:(i + 1) * P], sk_nat[:, 4 * j + i, :], ident[:, :])
                ins.then_inc(skT_done, 1)
            pe.wait_ge(values_ready, 4)
            pe.wait_ge(skT_ready, 4)

            def logits_of(n):
                q, k, b, r, _ = instance(n)
                if n >= 2:
                    pe.wait_ge(nmax_ready, n - 1)
                rows = slice(r, r + HEAD)
                mm(ps[n % 2][:, 0:P], qkT[rows, q, b, 0:P], qkT[rows, k, b, 0:P], start=True, stop=True)
                mm(ps[n % 2][:, P:3 * P], qkT[rows, q, b, P:SEQ], qkT[rows, k, b, :], start=True, stop=True)\
                    .then_inc(logits_done, 1)

            def probs_transposes(m):
                if m < MOBA_HEADS:
                    src = expd[:, m % 4, :]
                    pe.wait_ge(exp_done, m + 1)
                else:
                    src = mixed[:, m % 2, :]
                    pe.wait_ge(mixed_ready, m - MOBA_HEADS + 1)
                if m >= 2:
                    pe.wait_ge(probsT_ready, m - 1)
                for i in range(3):
                    ins = pe.transpose(ps[2 + m % 2][:, i * P:(i + 1) * P], src[:, i * P:(i + 1) * P], ident[:, :])
                ins.then_inc(probsT_done, 1)

            def values_of(m):
                pe.wait_ge(probsT_ready, m + 1)
                if m < MOBA_HEADS:
                    kind, bank, cols = 0, 4, slice(m * HEAD, (m + 1) * HEAD)
                else:
                    kind, bank, cols = 1, 6, slice((m - MOBA_HEADS) * P, (m - MOBA_HEADS + 1) * P)
                pT = probsT[:, m % 2, :]
                mm(ps[bank][:, cols], pT[:, 0:P], v_sb[:, kind, 0, cols], start=True, stop=True)
                mm(ps[bank + 1][:, cols], pT[:, P:2 * P], v_sb[:, kind, 0, cols], start=True, stop=False)
                mm(ps[bank + 1][:, cols], pT[:, 2 * P:3 * P], v_sb[:, kind, 1, cols], start=False, stop=True)\
                    .then_inc(heads_done, 1)

            n = 0
            for m in range(MIXES):
                while n < min(exps_for(m) + 2, INSTANCES):
                    logits_of(n)
                    n += 1
                probs_transposes(m)
                if m:
                    values_of(m - 1)
            values_of(MIXES - 1)

            pe.wait_ge(mix_ready, 4)
            feat_transposes(1, 0, None, None)
            pe.wait_ge(feat_ready, 8)
            for c in range(2):
                w = 6 + c
                pe.wait_ge(w_loaded[w % W_SLOTS], 16 * (w // W_SLOTS + 1))
                for h in range(HALVES):
                    y = ps[4 + 2 * h + c]
                    for k in range(KD):
                        mm(y[:, :], featT[:, k, h * P:(h + 1) * P], w_ring[:, w % W_SLOTS, k, :], start=k == 0, stop=False)
                    ins = mm(y[:, :], ident[:, :], x_sb[:, h, c * COLS:(c + 1) * COLS], start=False, stop=True)
                ins.then_inc(x2_done, 1)
                pe.wait_ge(x2_done, c + 1)
                pe.sem_inc(w_used, 1)
            pe.wait_ge(scaled_ready, 2 + 4)
            feat_transposes(2, 0, None, None)
            pe.wait_ge(feat_ready, 12)

            def key_scores(hp):
                pe.wait_ge(query_ready, hp + 1)
                if hp >= 2:
                    pe.wait_ge(scores_ready, hp - 1)
                for h in range(HALVES):
                    ins = mm(ps[hp % 2][:, h * P:(h + 1) * P], qT[:, hp % 2, h * P:(h + 1) * P], skT[:, hp, :],
                             start=True, stop=True)
                ins.then_inc(scores_done, 1)

            for hp in range(HP):
                w, c = 8 + hp // 4, hp % 4
                if c == 0:
                    pe.wait_ge(w_loaded[w % W_SLOTS], 16 * (w // W_SLOTS + 1))
                if hp >= 2:
                    pe.wait_ge(query_ready, hp - 1)
                for k in range(KD):
                    ins = mm(ps[2 + hp % 2][:, 0:SEQ], w_ring[:, w % W_SLOTS, k, c * P:(c + 1) * P], featT[:, k, :],
                             start=k == 0, stop=k == KD - 1)
                ins.then_inc(query_done, 1)
                if c == 3:
                    pe.wait_ge(query_done, hp + 1)
                    pe.sem_inc(w_used, 1)
                if hp:
                    key_scores(hp - 1)
            key_scores(HP - 1)
            for h in range(HALVES):
                pe.wait_ge(chosen_ready, h + 1)
                pe.wait_ge(scores_ready, HP)
                for a in range(3):
                    ins = pe.transpose(ps[h][:, a * P:(a + 1) * P], chosen[:, a, :], ident[:, :])
                ins.then_inc(routesT_done, 1)

            def gate_tokens(i, first):
                for b in range(2):
                    pe.wait_ge(hot_ready, 2 * i + (b + 1))
                    if not first:
                        pe.wait_ge(gate_ready, 2 * i + (b - 1))
                    for j in range(4):
                        ins = mm(ps[b][:, j * P:(j + 1) * P], hot2[:, 4 * b + j, :], hot1[:, 4 * b + j, :],
                                 start=True, stop=True)
                    ins.then_inc(gate_done, 1)

            pe.wait_ge(routes_ready, HALVES)
            gate_tokens(0, True)
            with pe.Fori(1, SEQ // TOK_STEP) as i:
                gate_tokens(i, False)

            def transposes(t, p, first=False):
                need(pe, u_loaded[p], (t - p) * 8 + 16)
                for b in range(2):
                    if not first:
                        need(pe, ut_lo_done, 2 * t + (b - 1))
                    for i in range(4):
                        k = 4 * b + i
                        ins = pe.transpose(ps[b][:, i * P:(i + 1) * P], u_raw[:, p, k * P:(k + 1) * P], ident[:, :])
                    ins.then_inc(ut_done, 1)

            def x_dot_u(t, p):
                need(pe, ut_lo_done, 2 * t + 2)
                need(pe, gelu_done, t - 1)
                for k in range(KD):
                    for n, (a, b) in enumerate(((ut_hi, xn_hi), (ut_hi, xn_lo), (ut_lo, xn_hi))):
                        ins = mm(ps[2 + p][:, 0:SEQ], a[:, p, k, :], b[:, k, :], start=k == 0 and n == 0,
                                 stop=k == KD - 1 and n == 2)
                ins.then_inc(h_done, 1)

            def times_v(t, p):
                need(pe, act_lo_done, t + 1)
                need(pe, v_lo_done, t + 1)
                for h in range(HALVES):
                    for a, b in ((act_hi, v_hi), (act_hi, v_lo), (act_lo, v_hi)):
                        for c in range(2):
                            ins = mm(ps[4 + 2 * h + c][:, :], a[:, p, h * P:(h + 1) * P], b[:, p, c * COLS:(c + 1) * COLS],
                                     start=False, stop=True, skip_group_check=True)
                ins.then_inc(v_used, 1)

            pe.wait_ge(gate_ready, SEQ // 4)
            pe.wait_ge(xn_lo_done, 4)
            transposes(0, 0, first=True)
            for p in range(2):
                transposes(p + 1, (p + 1) % 2)
                x_dot_u(p, p)
            with pe.Fori(0, (LAG - 2) // 2) as turn:
                s = turn * 2 + 2
                for p in range(2):
                    transposes(s + (p + 1), (p + 1) % 2)
                    x_dot_u(s + p, p)
            with pe.Fori(0, (TILES - 2 - LAG) // 2) as turn:
                s = turn * 2 + LAG
                for p in range(2):
                    transposes(s + (p + 1), (p + 1) % 2)
                    x_dot_u(s + p, p)
                    times_v(s + (p - LAG), p)
            for s in (TILES - 2, TILES - 1):
                if s + 1 < TILES:
                    transposes(s + 1, (s + 1) % 2)
                x_dot_u(s, s % 2)
                times_v(s - LAG, s % 2)
            with pe.Fori(0, LAG // 2) as turn:
                s = turn * 2 + (TILES - LAG)
                for p in range(2):
                    times_v(s + p, p)


_INS = ['x', 'norm1_g', 'w_in', 'moba_qk_norm_g', 'diff_qk_norm_g', 'diff_lambda', 'diff_subln_g', 'w_out', 'norm2_g',
        'peer_w_query', 'peer_sub_keys', 'peer_u', 'peer_v']


def kernel(**inputs):
    import numpy as _np
    import concourse.bacc as _bacc
    from concourse import mybir as _mybir
    from concourse.bass_utils import run_bass_kernel_spmd as _run

    nc = _bacc.Bacc("TRN2", target_bir_lowering=False, num_devices=1)
    arrays, args = {}, []
    for name in _INS:
        a = _np.ascontiguousarray(inputs[name])
        arrays[f"in_{name}_dram"] = a
        args.append(nc.dram_tensor(f"in_{name}_dram", a.shape, _mybir.dt.from_np(a.dtype), kind="ExternalInput").ap())
    args.append(nc.dram_tensor("out_0_dram", (1, SEQ, D), _mybir.dt.float32, kind="ExternalOutput").ap())
    layer(nc, *args)
    r = _run(nc, [arrays], core_ids=[0])
    return r.results[0]["out_0_dram"]
```

```python
import math
from contextlib import ExitStack

import concourse.bass as bass
from concourse import mybir

F32 = mybir.dt.float32
F32R = mybir.dt.float32r
U32 = mybir.dt.uint32
BF16 = mybir.dt.bfloat16
ALU = mybir.AluOpType
ACT = mybir.ActivationFunctionType
AX = mybir.AxisListType

P = 128
SEQ = 256
D = 1024
HALVES = SEQ // P
KD = D // P
HEAD = 64
MOBA_HEADS = 8
DIFF_HEADS = 4
COLS = 512
TOPK = 16
PEER_HEADS = 8
N_KEYS = 128
SLOTS = PEER_HEADS * TOPK
HP = PEER_HEADS * 2
TILES = N_KEYS
EPS = 1e-6
LAM_INIT = 0.8 - 0.6 * math.exp(-0.3 * 0)
MASKED = -1.0e30
REMOVED = -3.0e38
W_SLOTS = 4
TAIL_TILES = 4
GATE_TILES = 16
LAG = TAIL_TILES + GATE_TILES
CAND_ROWS = 17
BLOCK_ORDER = [0, 1, 3, 4, 2, 5]
QK_GROUPS = 4 * HALVES
GROUPS = 6 * HALVES
MOBA_N = MOBA_HEADS
INSTANCES = MOBA_HEADS + 2 * DIFF_HEADS
MIXES = MOBA_HEADS + DIFF_HEADS
TOK_STEP = 8
GROUP = 4
G1, G2, GQK, GSUB = 0, 8, 16, 20
N_GAINS = 21


def layer(nc, x, norm1_g, w_in, moba_g, diff_g, diff_lambda, subln_g, w_out, norm2_g, w_query, sub_keys,
          peer_u, peer_v, out):
    keep = ExitStack()

    base = (nc.sbuf_base + 31) // 32 * 32

    class Region:
        def __init__(self, at):
            self.at = at

        def put(self, name, shape, dt=F32):
            t = nc.alloc_sbuf_tensor_at(name, shape, dt, offset=self.at)
            size = 2 if dt == BF16 else 4
            for n in shape[1:]:
                size *= n
            self.at += (size + 31) // 32 * 32
            return t

    whole = Region(base)
    ident = whole.put("ident", [P, P])
    gains = whole.put("gains", [P, N_GAINS])
    routes = whole.put("routes", [P, 5, SEQ], BF16)
    xn_hi = whole.put("xn_hi", [P, KD, SEQ], F32R)
    xn_lo = whole.put("xn_lo", [P, KD, SEQ], F32R)
    stream_at = whole.at
    u_raw = whole.put("u_raw", [P, 2, D])
    v_raw = whole.put("v_raw", [P, 2, D])
    ut_hi_at = whole.at
    ut_hi = whole.put("ut_hi", [P, 2, KD, P], F32R)
    ut_lo = whole.put("ut_lo", [P, 2, KD, P], F32R)
    h_out = whole.put("h_out", [P, 2, SEQ])
    h_in = whole.put("h_in", [P, 2, SEQ])
    split_at = whole.at
    act_hi = whole.put("act_hi", [P, 2, SEQ], F32R)
    act_lo = whole.put("act_lo", [P, 2, SEQ], F32R)
    v_hi = whole.put("v_hi", [P, 2, D], F32R)
    v_lo = whole.put("v_lo", [P, 2, D], F32R)
    whole.at += 2048
    arena_at = whole.at
    gate_m = whole.put("gate_m", [P, SEQ, N_KEYS])

    over = Region(split_at)
    hot = over.put("hot", [P, 2, 2, N_KEYS, TOK_STEP], BF16)
    gated1 = over.put("gated1", [P, 2, 3, N_KEYS, TOK_STEP], BF16)
    key_no = over.put("key_no", [P, N_KEYS, TOK_STEP], BF16)
    assert over.at <= arena_at
    over = Region(ut_hi_at)
    ut_plain = over.put("ut_plain", [P, 2, KD, P])
    over = Region(split_at)
    qT = over.put("qT", [P, 2, SEQ])

    over = Region(arena_at)
    w_ring = over.put("w_ring", [P, W_SLOTS, KD, COLS])
    featT = over.put("featT", [P, KD, SEQ])
    skT = over.put("skT", [P, HP, N_KEYS])
    routing_at = over.at
    bias_t = over.put("bias_t", [P, MOBA_HEADS, 3 * P])
    v_sb = over.put("v_sb", [P, 2, HALVES, COLS])
    x_sb = over.put("x_sb", [P, HALVES, D])
    scaled = over.put("scaled", [P, HALVES, D])
    gain_rows = over.put("gain_rows", [N_GAINS, P])
    lam_in = over.put("lam_in", [P, 4 * HEAD])
    lam_prod = over.put("lam_prod", [P, 2, HEAD])
    tiny = {}
    for name, n in (("ssq", 2), ("ms", 2), ("sd", 2), ("rstd", 2), ("dots", 2), ("edots", 2), ("lam", 2),
                    ("qk_ss", 64), ("qk_ms", 64), ("qk_sd", 64), ("qk_rs", 64), ("nmax", 32), ("sums", 32),
                    ("rsum", 32), ("rlam", 8), ("d_ss", 8), ("d_ms", 8), ("d_sd", 8), ("d_rs", 8),
                    ("ssq2", 4), ("ms2", 2), ("sd2", 2), ("rstd2", 2), ("ssq2s", 2)):
        tiny[name] = over.put("t_" + name, [P, n])
    assert over.at <= arena_at + 4 * SEQ * N_KEYS

    over = Region(stream_at)
    qkT = over.put("qkT", [P, 4, 4, SEQ])
    sk_nat = over.put("sk_nat", [P, HP, P])
    normed = over.put("normed", [P, 2, COLS])
    squares = over.put("squares", [P, 2, COLS])
    logits = over.put("logits", [P, 2, 3 * P])
    expd = over.put("expd", [P, 4, 3 * P])
    mixed = over.put("mixed", [P, 2, 3 * P])
    probsT = over.put("probsT", [P, 2, 3 * P])
    assert over.at <= arena_at - 2048 - 2048
    over = Region(routing_at)
    scores = over.put("scores", [P, HALVES, HP, N_KEYS])
    key_val = over.put("key_val", [P, HALVES, HP, TOPK])
    key_idx = over.put("key_idx", [P, HALVES, HP, TOPK], U32)
    cand = over.put("cand", [P, 2, HALVES, CAND_ROWS * 8])
    best = over.put("best", [P, HALVES, PEER_HEADS, TOPK])
    pos = over.put("pos", [P, HALVES, PEER_HEADS, TOPK], U32)
    key_idb = over.put("key_idb", [P, 2, TOPK, HALVES, GROUP], BF16)
    pos_u = over.put("pos_u", [P, 2, TOPK, HALVES, GROUP], U32)
    pos_b = over.put("pos_b", [P, 3, TOPK, HALVES, GROUP], BF16)
    match = over.put("match", [P, 2, TOPK, HALVES * GROUP * TOPK], BF16)
    iota16 = over.put("iota16", [P, TOPK, HALVES * GROUP * TOPK], BF16)
    chosen = over.put("chosen", [P, HALVES, 3, SLOTS])
    gexp = over.put("gexp", [P, HALVES, PEER_HEADS, TOPK])
    gsum = over.put("gsum", [P, 2, HALVES, PEER_HEADS])
    rest = over.put("rest", [P, 2, SEQ])
    assert over.at <= arena_at + 4 * SEQ * N_KEYS

    with keep:
        h_spill = nc.dram_tensor("h_spill", (TILES, P, SEQ), F32, kind="Internal").ap()
        ps = [keep.enter_context(nc.psum_tensor(f"bank{i}", [P, COLS], F32)) for i in range(8)]

        def sem(name):
            return keep.enter_context(nc.semaphore(name))

        x_loaded = [sem(f"x_loaded{h}") for h in range(HALVES)]
        gains_loaded = sem("gains_loaded")
        lam_loaded = sem("lam_loaded")
        sk_loaded = sem("sk_loaded")
        w_loaded = [sem(f"w_loaded{i}") for i in range(W_SLOTS)]
        u_loaded = [sem(f"u_loaded{i}") for i in range(2)]
        v_loaded = [sem(f"v_loaded{i}") for i in range(2)]
        h_stored = [sem(f"h_stored{i}") for i in range(2)]
        h_loaded = [sem(f"h_loaded{i}") for i in range(2)]
        stored = sem("stored")
        ident_ready = sem("ident_ready")
        pool_step = sem("pool_step")
        bias_ready = sem("bias_ready")
        iota_ready = sem("iota_ready")
        dve_step = sem("dve_step")
        gainsT_done = sem("gainsT_done")
        gains_ready = sem("gains_ready")
        ssq_done = sem("ssq_done")
        ms_ready = sem("ms_ready")
        sd_ready = sem("sd_ready")
        scaled_ready = sem("scaled_ready")
        feat_done = sem("feat_done")
        feat_ready = sem("feat_ready")
        proj_done = sem("proj_done")
        w_used = sem("w_used")
        sq_done = sem("sq_done")
        qk_ms_ready = sem("qk_ms_ready")
        qk_sd_ready = sem("qk_sd_ready")
        normed_ready = sem("normed_ready")
        qkT_done = sem("qkT_done")
        qkT_ready = sem("qkT_ready")
        values_ready = sem("values_ready")
        skT_done = sem("skT_done")
        skT_ready = sem("skT_ready")
        logits_done = sem("logits_done")
        nmax_ready = sem("nmax_ready")
        exp_done = sem("exp_done")
        mixed_ready = sem("mixed_ready")
        probsT_done = sem("probsT_done")
        probsT_ready = sem("probsT_ready")
        heads_done = sem("heads_done")
        dots_ready = sem("dots_ready")
        edots_ready = sem("edots_ready")
        d_sq_done = sem("d_sq_done")
        d_ms_ready = sem("d_ms_ready")
        d_sd_ready = sem("d_sd_ready")
        mix_ready = sem("mix_ready")
        x2_done = sem("x2_done")
        xn_full = sem("xn_full")
        xn_hi_done = sem("xn_hi_done")
        xn_lo_done = sem("xn_lo_done")
        query_done = sem("query_done")
        query_ready = sem("query_ready")
        scores_done = sem("scores_done")
        scores_ready = sem("scores_ready")
        chosen_ready = sem("chosen_ready")
        routesT_done = sem("routesT_done")
        routes_ready = sem("routes_ready")
        gexp_in = sem("gexp_in")
        gexp_done = sem("gexp_done")
        hot_ready = sem("hot_ready")
        gate_done = sem("gate_done")
        gate_ready = sem("gate_ready")
        ut_done = sem("ut_done")
        ut_hi_done = sem("ut_hi_done")
        ut_lo_done = sem("ut_lo_done")
        h_done = sem("h_done")
        gelu_done = sem("gelu_done")
        act_done = sem("act_done")
        act_hi_done = sem("act_hi_done")
        act_lo_done = sem("act_lo_done")
        v_hi_done = sem("v_hi_done")
        v_lo_done = sem("v_lo_done")
        v_used = sem("v_used")
        y_ready = sem("y_ready")

        def need(eng, s, value):
            if not isinstance(value, int) or value > 0:
                eng.wait_ge(s, value)

        def w_source(w):
            if w < 6:
                m, c = w_in, BLOCK_ORDER[w]
            elif w < 8:
                m, c = w_out, w - 6
            else:
                m, c = w_query, w - 8
            return m[0, :, c * COLS:(c + 1) * COLS].rearrange("(k p) n -> p k n", p=P)

        def instance(n):
            if n < MOBA_HEADS:
                return 0, 1, n // 2, HEAD * (n % 2), n
            i, j = divmod(n - MOBA_HEADS, 2)
            return 2, 3, i, HEAD * j, 2 * i + 1

        def exps_for(m):
            return m + 1 if m < MOBA_HEADS else MOBA_HEADS + 2 * (m - MOBA_HEADS) + 2

        block = keep.enter_context(nc.Block())

        @block.sync
        def _(sp):
            for h in range(HALVES):
                sp.dma_start(x_sb[:, h, :], x[0, h * P:(h + 1) * P, :]).then_inc(x_loaded[h], 16)
            sp.dma_start(w_ring[:, 0, :, :], w_source(0)).then_inc(w_loaded[0], 16)
            rows = [(G1, KD, norm1_g[0].rearrange("(r c) -> r c", c=P)), (G2, KD, norm2_g[0].rearrange("(r c) -> r c", c=P)),
                    (GSUB, 1, subln_g)]
            for r, n, src in rows:
                sp.dma_start(gain_rows[r:r + n, :], src).then_inc(gains_loaded, 16)
            for r, src in ((GQK, moba_g[0]), (GQK + 2, diff_g[0])):
                for c in range(2):
                    sp.dma_start(gain_rows[r:r + 2, c * HEAD:(c + 1) * HEAD], src).then_inc(gains_loaded, 16)
            sp.dma_start(lam_in[:, :], diff_lambda.rearrange("a b c -> a (b c)").to_broadcast([P, 4 * HEAD]))\
              .then_inc(lam_loaded, 16)
            for w in range(1, 12):
                if w >= W_SLOTS:
                    sp.wait_ge(w_used, w - W_SLOTS + 1)
                sp.dma_start(w_ring[:, w % W_SLOTS, :, :], w_source(w)).then_inc(w_loaded[w % W_SLOTS], 16)
                if w == 3:
                    sp.dma_start(sk_nat[:, :, :], sub_keys[0].rearrange("h a n d -> n (h a) d")).then_inc(sk_loaded, 16)

            def load_u(t, p, held=True):
                if held:
                    sp.wait_ge(ut_done, 2 * t - 2)
                sp.dma_start(u_raw[:, p, :], peer_u[0, bass.ds(t * P, P), :]).then_inc(u_loaded[p], 16)

            def load_v(t, p, held=True):
                if held:
                    sp.wait_ge(v_lo_done, t - 1)
                sp.dma_start(v_raw[:, p, :], peer_v[0, bass.ds(t * P, P), :]).then_inc(v_loaded[p], 16)

            def store_h(t, p):
                sp.wait_ge(gelu_done, t + 1)
                sp.dma_start(h_spill[bass.ds(t, 1), :, :].rearrange("a p c -> (a p) c"), h_out[:, p, :])\
                  .then_inc(h_stored[p], 16)

            def load_h(t, p, held=True):
                if held:
                    sp.wait_ge(act_lo_done, t - 1)
                sp.wait_ge(h_stored[p], (t - p) * 8 + 16)
                sp.dma_start(h_in[:, p, :], h_spill[bass.ds(t, 1), :, :].rearrange("a p c -> (a p) c"))\
                  .then_inc(h_loaded[p], 16)

            sp.wait_ge(feat_done, 8)
            load_u(0, 0, False)
            load_u(1, 1, False)
            load_v(0, 0, False)
            load_v(1, 1, False)
            load_u(2, 0)
            load_u(3, 1)
            store_h(0, 0)
            store_h(1, 1)
            with sp.Fori(0, (LAG - 2) // 2) as turn:
                t = turn * 2 + 4
                for p in range(2):
                    load_u(t + p, p)
                    store_h(t + (p - 2), p)
            for p in range(2):
                load_h(p, p, False)
            with sp.Fori(0, (TILES - LAG - 2) // 2) as turn:
                t = turn * 2 + (LAG + 2)
                for p in range(2):
                    load_u(t + p, p)
                    store_h(t + (p - 2), p)
                    load_h(t + (p - LAG), p)
                    load_v(t + (p - LAG), p)
            for t in range(TILES, TILES + 2):
                store_h(t - 2, t % 2)
                load_h(t - LAG, t % 2)
                load_v(t - LAG, t % 2)
            with sp.Fori(0, (LAG - 2) // 2) as turn:
                t = turn * 2 + (TILES + 2 - LAG)
                for p in range(2):
                    load_h(t + p, p)
                    load_v(t + p, p)
            sp.wait_ge(y_ready, 4)
            for h in range(HALVES):
                sp.dma_start(out[0, h * P:(h + 1) * P, :], gate_m[:, 8 * h:8 * h + 8, :].rearrange("p a b -> p (a b)"))\
                  .then_inc(stored, 16)
            sp.wait_ge(stored, 16 * HALVES)

        @block.gpsimd
        def _(pool):
            pool.memset(ident[:, :], 0.0).then_inc(pool_step, 1)
            pool.wait_ge(pool_step, 1)
            pool.affine_select(out=ident[:, :], in_=ident[:, :], compare_op=ALU.not_equal, fill=1.0, base=0,
                               pattern=[[-1, P]], channel_multiplier=1).then_inc(ident_ready, 1)
            dist = bias_t[:, 0, :]
            pool.iota(dist[:, 0:P], pattern=[[1, P]], base=0, channel_multiplier=-1,
                      allow_small_or_imprecise_dtypes=True).then_inc(pool_step, 1)
            pool.iota(dist[:, P:3 * P], pattern=[[1, 2 * P]], base=-P, channel_multiplier=-1,
                      allow_small_or_imprecise_dtypes=True).then_inc(pool_step, 1)
            pool.wait_ge(pool_step, 3)
            for h in range(MOBA_HEADS - 1, -1, -1):
                if h == 0:
                    pool.wait_ge(pool_step, 3 + MOBA_HEADS - 1)
                pool.tensor_scalar(bias_t[:, h, :], dist[:, :], 2.0 ** -(h + 1), None, ALU.mult).then_inc(pool_step, 1)
            pool.wait_ge(pool_step, 3 + MOBA_HEADS)
            pool.affine_select(out=bias_t[:, :, 0:P], in_=bias_t[:, :, 0:P], compare_op=ALU.is_ge, fill=MASKED,
                               base=0, pattern=[[0, MOBA_HEADS], [-1, P]], channel_multiplier=1)\
                .then_inc(bias_ready, 1)
            pool.affine_select(out=bias_t[:, :, P:3 * P], in_=bias_t[:, :, P:3 * P], compare_op=ALU.is_ge, fill=MASKED,
                               base=P, pattern=[[0, MOBA_HEADS], [-1, 2 * P]], channel_multiplier=1)\
                .then_inc(bias_ready, 1)
            pool.wait_ge(feat_done, 12)
            pool.iota(iota16[:, :, :], pattern=[[1, TOPK], [0, HALVES * GROUP * TOPK]], base=0, channel_multiplier=0,
                      allow_small_or_imprecise_dtypes=True).then_inc(iota_ready, 1)
            pool.iota(key_no[:, :, :], pattern=[[1, N_KEYS], [0, TOK_STEP]], base=0, channel_multiplier=0,
                      allow_small_or_imprecise_dtypes=True).then_inc(iota_ready, 1)

        @block.scalar
        def _(act):
            for h in range(HALVES):
                act.wait_ge(x_loaded[h], 16)
                act.activation(scaled[:, h, :], x_sb[:, h, :], ACT.Square, accum_out=tiny["ssq"][:, h:h + 1])\
                   .then_inc(ssq_done, 1)
            act.wait_ge(gainsT_done, 1)
            act.activation(gains[:, :], ps[5][:, 0:N_GAINS], ACT.Copy).then_inc(gains_ready, 1)
            act.wait_ge(ms_ready, 1)
            act.activation(tiny["sd"][:, :], tiny["ms"][:, :], ACT.Sqrt).then_inc(sd_ready, 1)
            act.wait_ge(gains_ready, 1)
            act.activation(gains[:, GQK:GQK + 3:2], gains[:, GQK:GQK + 3:2], ACT.Copy, scale=HEAD ** -0.5)\
               .then_inc(gains_ready, 1)
            act.activation(gains[:, GSUB:GSUB + 1], gains[:, GSUB:GSUB + 1], ACT.Copy, scale=1.0 - LAM_INIT)\
               .then_inc(gains_ready, 1)
            act.wait_ge(gains_ready, 3)

            def feat_evac(rnd, pair, bank, gain):
                act.wait_ge(feat_done, rnd * 4 + pair + 1)
                for i in range(2):
                    k = 2 * pair + i
                    ins = act.activation(featT[:, k, :], ps[bank][:, i * SEQ:(i + 1) * SEQ], ACT.Copy,
                                         scale=1.0 if gain(k) is None else gain(k))
                ins.then_inc(feat_ready, 1)

            for pair in range(4):
                feat_evac(0, pair, 6 + pair % 2, lambda k: gains[:, G1 + k:G1 + k + 1])

            def qkT_evac(g):
                b, h = divmod(g, HALVES)
                act.wait_ge(qkT_done, g + 1)
                act.activation(qkT[:, b, :, h * P:(h + 1) * P], ps[4 + g % 2][:, :].rearrange("p (b t) -> p b t", b=4),
                               ACT.Copy, scale=gains[:, GQK + b:GQK + b + 1]).then_inc(qkT_ready, 1)

            for g in range(GROUPS):
                if g < QK_GROUPS:
                    act.wait_ge(proj_done, g + 1)
                    if g >= 2:
                        act.wait_ge(qk_ms_ready, g - 1)
                    act.activation(squares[:, g % 2, :], ps[g % 4][:, :], ACT.Square).then_inc(sq_done, 1)
                    act.wait_ge(qk_ms_ready, g + 1)
                    act.activation(tiny["qk_sd"][:, 8 * g:8 * g + 8], tiny["qk_ms"][:, 8 * g:8 * g + 8], ACT.Sqrt)\
                       .then_inc(qk_sd_ready, 1)
                if 1 <= g <= QK_GROUPS:
                    qkT_evac(g - 1)
                if g >= QK_GROUPS:
                    i, h = divmod(g - QK_GROUPS, HALVES)
                    act.wait_ge(proj_done, g + 1)
                    act.activation(v_sb[:, i, h, :], ps[g % 4][:, :], ACT.Copy).then_inc(values_ready, 1)
            for j in range(4):
                act.wait_ge(skT_done, j + 1)
                act.activation(skT[:, 4 * j:4 * j + 4, :], ps[4 + j % 2][:, :].rearrange("p (a n) -> p a n", a=4), ACT.Copy)\
                   .then_inc(skT_ready, 1)
            act.wait_ge(dots_ready, 2)
            act.activation(tiny["edots"][:, :], tiny["dots"][:, :], ACT.Exp).then_inc(edots_ready, 1)

            def exps(n):
                act.wait_ge(nmax_ready, n + 1)
                if n >= 4:
                    if n < 12:
                        act.wait_ge(probsT_done, n - 3)
                    else:
                        act.wait_ge(mixed_ready, (n - 12) // 2 + 1)
                for h, lo, hi in ((0, 0, P), (1, P, 3 * P)):
                    c = h * INSTANCES + n
                    ins = act.activation(expd[:, n % 4, lo:hi], logits[:, n % 2, lo:hi], ACT.Exp,
                                         bias=tiny["nmax"][:, c:c + 1], accum_out=tiny["sums"][:, c:c + 1])
                ins.then_inc(exp_done, 1)

            def probs_evac(m):
                act.wait_ge(probsT_done, m + 1)
                if m >= 2:
                    act.wait_ge(heads_done, m - 1)
                act.activation(probsT[:, m % 2, :], ps[2 + m % 2][:, 0:3 * P], ACT.Copy).then_inc(probsT_ready, 1)

            n = 0
            for m in range(MIXES):
                while n < min(exps_for(m) + 1, INSTANCES):
                    exps(n)
                    n += 1
                probs_evac(m)
            act.wait_ge(heads_done, MIXES)
            for h in range(HALVES):
                act.activation(squares[:, h, :], ps[6 + h][:, :], ACT.Square).then_inc(d_sq_done, 1)
            act.wait_ge(d_ms_ready, 1)
            act.activation(tiny["d_sd"][:, :], tiny["d_ms"][:, :], ACT.Sqrt).then_inc(d_sd_ready, 1)
            for pair in range(4):
                feat_evac(1, pair, pair % 2, lambda k: None if k < 4 else gains[:, GSUB:GSUB + 1])
            for h in range(HALVES):
                for c in range(2):
                    act.wait_ge(x2_done, c + 1)
                    act.activation(scaled[:, h, c * COLS:(c + 1) * COLS], ps[4 + 2 * h + c][:, :], ACT.Square,
                                   accum_out=tiny["ssq2"][:, 2 * h + c:2 * h + c + 1]).then_inc(ssq_done, 1)
            act.wait_ge(ms_ready, 2)
            act.activation(tiny["sd2"][:, :], tiny["ms2"][:, :], ACT.Sqrt).then_inc(sd_ready, 1)
            for pair in range(4):
                feat_evac(2, pair, pair % 2, lambda k: gains[:, G2 + k:G2 + k + 1])
                act.wait_ge(feat_ready, 8 + pair + 1)
                act.activation(xn_hi[:, 2 * pair:2 * pair + 2, :], featT[:, 2 * pair:2 * pair + 2, :], ACT.Copy)\
                   .then_inc(xn_hi_done, 1)

            def scores_evac(hp):
                act.wait_ge(scores_done, hp + 1)
                act.activation(scores[:, :, hp, :], ps[hp % 2][:, 0:SEQ].rearrange("p (h n) -> p h n", h=2), ACT.Copy)\
                   .then_inc(scores_ready, 1)

            for hp in range(HP):
                act.wait_ge(query_done, hp + 1)
                if hp >= 2:
                    act.wait_ge(scores_done, hp - 1)
                act.activation(qT[:, hp % 2, :], ps[2 + hp % 2][:, 0:SEQ], ACT.Copy).then_inc(query_ready, 1)
                if hp >= 1:
                    scores_evac(hp - 1)
            scores_evac(HP - 1)
            def ut_split_half(t, p, b):
                need(act, ut_done, 2 * t + (b + 1))
                if b == 0:
                    need(act, h_done, t - 1)
                act.activation(ut_hi[:, p, 4 * b:4 * b + 4, :].rearrange("p a b -> p (a b)"), ps[b][:, :], ACT.Copy)\
                   .then_inc(ut_hi_done, 1)

            def ut_split(t, p):
                ut_split_half(t, p, 0)
                ut_split_half(t, p, 1)

            def gelu(t, p, bank):
                need(act, h_done, t + 1)
                need(act, h_stored[p], (t - p) * 8)
                act.activation(h_out[:, p, :], ps[bank][:, 0:SEQ], ACT.Gelu).then_inc(gelu_done, 1)

            def v_split(t, p):
                need(act, act_done, t + 1)
                need(act, v_used, t - 1)
                act.activation(act_hi[:, p, :], h_in[:, p, :], ACT.Copy).then_inc(act_hi_done, 1)
                need(act, v_loaded[p], (t - p) * 8 + 16)
                act.activation(v_hi[:, p, :], v_raw[:, p, :], ACT.Copy).then_inc(v_hi_done, 1)

            def ut_copy(t, p):
                for b in range(2):
                    need(act, ut_done, 2 * t + (b + 1))
                    if b == 0:
                        need(act, h_done, t - 1)
                    act.activation(ut_plain[:, p, 4 * b:4 * b + 4, :].rearrange("p a b -> p (a b)"), ps[b][:, :], ACT.Copy)\
                       .then_inc(ut_hi_done, 1)

            ut_copy(0, 0)
            for s in range(TAIL_TILES):
                t = s + 1
                if t < TAIL_TILES:
                    ut_copy(t, t % 2)
                else:
                    ut_split(t, t % 2)
                gelu(s, s % 2, 2)
                if s == 0:
                    act.wait_ge(gexp_in, 1)
                    act.activation(gexp[:, :, :, :], gexp[:, :, :, :], ACT.Exp).then_inc(gexp_done, 1)

            def gate_evac(i, n):
                act.wait_ge(gate_done, 4 * i + (n + 1))
                act.activation(gate_m[:, bass.ds(i * 16 + 4 * n, 4), :].rearrange("p a b -> p (a b)"), ps[3][:, :],
                               ACT.Copy).then_inc(gate_ready, 1)

            def gate_step(i, p, first):
                s = i + TAIL_TILES
                if not first:
                    gate_evac(i - 1, 2)
                ut_split_half(s + 1, 1 - p, 0)
                if not first:
                    gate_evac(i - 1, 3)
                ut_split_half(s + 1, 1 - p, 1)
                gate_evac(i, 0)
                gate_evac(i, 1)
                gelu(s, p, 2)

            gate_step(0, 0, True)
            gate_step(1, 1, False)
            with act.Fori(0, GATE_TILES // 2 - 1) as turn:
                for p in range(2):
                    gate_step(turn * 2 + (2 + p), p, False)
            gate_evac(GATE_TILES - 1, 2)
            gate_evac(GATE_TILES - 1, 3)
            v_split(0, 0)
            with act.Fori(0, (TILES - LAG - 2) // 2) as turn:
                for p in range(2):
                    s = turn * 2 + (LAG + p)
                    ut_split(s + 1, 1 - p)
                    v_split(s - (LAG - 1), 1 - p)
                    gelu(s, p, 2 + p)
            for s in range(TILES - 2, TILES):
                if s + 1 < TILES:
                    ut_split(s + 1, (s + 1) % 2)
                v_split(s - (LAG - 1), (s + 1) % 2)
                gelu(s, s % 2, 2 + s % 2)
            with act.Fori(0, (LAG - 2) // 2) as turn:
                for p in range(2):
                    v_split(turn * 2 + (TILES - LAG + 1 + p), 1 - p)
            v_split(TILES - 1, 1)
            act.wait_ge(v_used, TILES)
            for c in range(2):
                act.activation(gate_m[:, 4 * c:4 * c + 4, :].rearrange("p a b -> p (a b)"), ps[4 + c][:, :], ACT.Copy)\
                   .then_inc(y_ready, 1)

        @block.vector
        def _(dve):
            steps = [0]

            def mark(ins):
                steps[0] += 1
                ins.then_inc(dve_step, 1)
                return steps[0]

            def link(ins):
                dve.wait_ge(dve_step, mark(ins))

            dve.wait_ge(ssq_done, 2)
            dve.tensor_scalar(tiny["ms"][:, :], tiny["ssq"][:, :], 1.0 / D, EPS, ALU.mult, ALU.add).then_inc(ms_ready, 1)
            dve.wait_ge(sd_ready, 1)
            link(dve.reciprocal(tiny["rstd"][:, :], tiny["sd"][:, :]))
            for h in range(HALVES):
                dve.tensor_scalar(scaled[:, h, :], x_sb[:, h, :], tiny["rstd"][:, h:h + 1], None, ALU.mult)\
                   .then_inc(scaled_ready, 1)
            dve.wait_ge(lam_loaded, 16)
            for i in range(2):
                dve.tensor_tensor_reduce(out=lam_prod[:, i, :], in0=lam_in[:, 2 * i * HEAD:(2 * i + 1) * HEAD],
                                         in1=lam_in[:, (2 * i + 1) * HEAD:(2 * i + 2) * HEAD], scale=1.0, scalar=0.0,
                                         op0=ALU.mult, op1=ALU.add, accum_out=tiny["dots"][:, i:i + 1])\
                   .then_inc(dots_ready, 1)
            for g in range(QK_GROUPS):
                cols = slice(8 * g, 8 * g + 8)
                dve.wait_ge(sq_done, g + 1)
                link(dve.tensor_reduce(tiny["qk_ss"][:, cols], squares[:, g % 2, :].rearrange("p (h d) -> p h d", d=HEAD),
                                       AX.X, ALU.add))
                dve.tensor_scalar(tiny["qk_ms"][:, cols], tiny["qk_ss"][:, cols], 1.0 / HEAD, EPS, ALU.mult, ALU.add)\
                   .then_inc(qk_ms_ready, 1)
                dve.wait_ge(qk_sd_ready, g + 1)
                link(dve.reciprocal(tiny["qk_rs"][:, cols], tiny["qk_sd"][:, cols]))
                if g >= 2:
                    dve.wait_ge(qkT_done, g - 1)
                dve.tensor_tensor(normed[:, g % 2, :].rearrange("p (h d) -> p h d", d=HEAD),
                                  ps[g % 4][:, :].rearrange("p (h d) -> p h d", d=HEAD),
                                  tiny["qk_rs"][:, cols].unsqueeze(2).to_broadcast([P, 8, HEAD]), ALU.mult)\
                   .then_inc(normed_ready, 1)
            dve.wait_ge(edots_ready, 1)
            link(dve.tensor_tensor(tiny["lam"][:, 0:1], tiny["edots"][:, 0:1], tiny["edots"][:, 1:2], ALU.subtract))
            link(dve.tensor_scalar(tiny["lam"][:, 1:2], tiny["lam"][:, 0:1], LAM_INIT, None, ALU.add))
            dve.wait_ge(bias_ready, 2)

            def bias_and_max(n):
                table = instance(n)[4]
                dve.wait_ge(logits_done, n + 1)
                if n >= 2:
                    dve.wait_ge(exp_done, n - 1)
                link(dve.tensor_tensor(logits[:, n % 2, :], ps[n % 2][:, 0:3 * P], bias_t[:, table, :], ALU.add))
                for h, lo, hi in ((0, 0, P), (1, P, 3 * P)):
                    c = h * INSTANCES + n
                    ins = dve.tensor_reduce(tiny["nmax"][:, c:c + 1], logits[:, n % 2, lo:hi], AX.X, ALU.max, negate=True)
                ins.then_inc(nmax_ready, 1)

            def mix_diff(i):
                n = MOBA_HEADS + 2 * i
                dve.wait_ge(exp_done, n + 2)
                if i >= 2:
                    dve.wait_ge(probsT_done, MOBA_HEADS + i - 1)
                for h in range(HALVES):
                    c = h * INSTANCES + n
                    ins = dve.reciprocal(tiny["rsum"][:, c:c + 2], tiny["sums"][:, c:c + 2])
                    at = mark(ins)
                dve.wait_ge(dve_step, at)
                for h in range(HALVES):
                    c = h * INSTANCES + n
                    at = mark(dve.tensor_scalar(tiny["rlam"][:, 2 * i + h:2 * i + h + 1], tiny["rsum"][:, c + 1:c + 2],
                                                tiny["lam"][:, 1:2], None, ALU.mult))
                dve.wait_ge(dve_step, at)
                for h, lo, hi in ((0, 0, P), (1, P, 3 * P)):
                    at = mark(dve.tensor_scalar(expd[:, (n + 1) % 4, lo:hi], expd[:, (n + 1) % 4, lo:hi],
                                                tiny["rlam"][:, 2 * i + h:2 * i + h + 1], None, ALU.mult))
                dve.wait_ge(dve_step, at)
                for h, lo, hi in ((0, 0, P), (1, P, 3 * P)):
                    c = h * INSTANCES + n
                    ins = dve.scalar_tensor_tensor(mixed[:, i % 2, lo:hi], expd[:, n % 4, lo:hi], tiny["rsum"][:, c:c + 1],
                                                   expd[:, (n + 1) % 4, lo:hi], ALU.mult, ALU.subtract)
                ins.then_inc(mixed_ready, 1)

            n = 0
            for m in range(MIXES):
                while n < min(exps_for(m) + 2, INSTANCES):
                    bias_and_max(n)
                    n += 1
                if m >= MOBA_HEADS:
                    mix_diff(m - MOBA_HEADS)
            dve.wait_ge(heads_done, MOBA_HEADS)
            for h in range(HALVES):
                c = h * INSTANCES
                at = mark(dve.reciprocal(tiny["rsum"][:, c:c + MOBA_HEADS], tiny["sums"][:, c:c + MOBA_HEADS]))
            dve.wait_ge(dve_step, at)
            for h in range(HALVES):
                c = h * INSTANCES
                dve.tensor_tensor(scaled[:, h, 0:COLS].rearrange("p (h d) -> p h d", d=HEAD),
                                  ps[4 + h][:, :].rearrange("p (h d) -> p h d", d=HEAD),
                                  tiny["rsum"][:, c:c + MOBA_HEADS].unsqueeze(2).to_broadcast([P, MOBA_HEADS, HEAD]),
                                  ALU.mult).then_inc(mix_ready, 1)
            for h in range(HALVES):
                dve.wait_ge(d_sq_done, h + 1)
                at = mark(dve.tensor_reduce(tiny["d_ss"][:, 4 * h:4 * h + 4],
                                            squares[:, h, :].rearrange("p (h d) -> p h d", d=P), AX.X, ALU.add))
            dve.wait_ge(dve_step, at)
            dve.tensor_scalar(tiny["d_ms"][:, :], tiny["d_ss"][:, :], 1.0 / P, EPS, ALU.mult, ALU.add).then_inc(d_ms_ready, 1)
            dve.wait_ge(d_sd_ready, 1)
            link(dve.reciprocal(tiny["d_rs"][:, :], tiny["d_sd"][:, :]))
            for h in range(HALVES):
                dve.tensor_tensor(scaled[:, h, COLS:D].rearrange("p (h d) -> p h d", d=P),
                                  ps[6 + h][:, :].rearrange("p (h d) -> p h d", d=P),
                                  tiny["d_rs"][:, 4 * h:4 * h + 4].unsqueeze(2).to_broadcast([P, DIFF_HEADS, P]),
                                  ALU.mult).then_inc(mix_ready, 1)
            dve.wait_ge(ssq_done, 2 + 4)
            link(dve.tensor_reduce(tiny["ssq2s"][:, :], tiny["ssq2"][:, :].rearrange("p (h c) -> p h c", c=2), AX.X, ALU.add))
            dve.tensor_scalar(tiny["ms2"][:, :], tiny["ssq2s"][:, :], 1.0 / D, EPS, ALU.mult, ALU.add).then_inc(ms_ready, 1)
            dve.wait_ge(sd_ready, 2)
            link(dve.reciprocal(tiny["rstd2"][:, :], tiny["sd2"][:, :]))
            for h in range(HALVES):
                for c in range(2):
                    ins = dve.tensor_scalar(scaled[:, h, c * COLS:(c + 1) * COLS], ps[4 + 2 * h + c][:, :],
                                            tiny["rstd2"][:, h:h + 1], None, ALU.mult)
                    ins.then_inc(scaled_ready, 1)
            for pair in range(4):
                dve.wait_ge(xn_hi_done, pair + 1)
                dve.tensor_tensor(xn_lo[:, 2 * pair:2 * pair + 2, :], featT[:, 2 * pair:2 * pair + 2, :],
                                  xn_hi[:, 2 * pair:2 * pair + 2, :].bitcast(F32), ALU.subtract).then_inc(xn_lo_done, 1)

            def top_keys(hp):
                dve.wait_ge(scores_ready, hp + 1)
                at = [0, 0]
                for r in range(2):
                    val = [key_val[:, h, hp, 8 * r:8 * r + 8] for h in range(HALVES)]
                    for h in range(HALVES):
                        if r:
                            dve.wait_ge(dve_step, at[h])
                        at[h] = mark(dve.max(val[h], scores[:, h, hp, :]))
                    for h in range(HALVES):
                        dve.wait_ge(dve_step, at[h])
                        last = mark(dve.max_index(key_idx[:, h, hp, 8 * r:8 * r + 8], val[h], scores[:, h, hp, :]))
                        if r == 0:
                            at[h] = mark(dve.match_replace(scores[:, h, hp, :], val[h], scores[:, h, hp, :], REMOVED))
                dve.wait_ge(dve_step, last)

            def top_candidates(i):
                v1, v2 = key_val[:, :, 2 * i, :], key_val[:, :, 2 * i + 1, :]
                mark(dve.tensor_tensor(cand[:, i % 2, :, 0:TOPK], v1[:, :, 0:1].to_broadcast([P, HALVES, TOPK]), v2, ALU.add))
                grid = [P, HALVES, TOPK - 1, 8]
                link(dve.tensor_tensor(cand[:, i % 2, :, TOPK:].rearrange("p h (a b) -> p h a b", b=8),
                                       v1[:, :, 1:].unsqueeze(3).to_broadcast(grid),
                                       v2[:, :, 0:8].unsqueeze(2).to_broadcast(grid), ALU.add))
                at = [0, 0]
                for r in range(2):
                    top = slice(8 * r, 8 * r + 8)
                    for h in range(HALVES):
                        if r:
                            dve.wait_ge(dve_step, at[h])
                        at[h] = mark(dve.max(best[:, h, i, top], cand[:, i % 2, h, :]))
                    for h in range(HALVES):
                        dve.wait_ge(dve_step, at[h])
                        last = mark(dve.max_index(pos[:, h, i, top], best[:, h, i, top], cand[:, i % 2, h, :]))
                        if r == 0:
                            at[h] = mark(dve.match_replace(cand[:, i % 2, h, :], best[:, h, i, top], cand[:, i % 2, h, :],
                                                           REMOVED))
                dve.wait_ge(dve_step, last)

            def resolve(q):
                heads = slice(GROUP * q, GROUP * q + GROUP)
                for a in range(2):
                    for h in range(HALVES):
                        mark(dve.tensor_copy(key_idb[:, a, :, h, :],
                                             key_idx[:, h, 2 * GROUP * q + a:2 * GROUP * (q + 1):2, :]
                                             .rearrange("p g k -> p k g")))
                where = pos[:, :, heads, :].rearrange("p h g s -> p s h g")
                mark(dve.tensor_scalar(pos_u[:, 0, :, :, :], where, 3, None, ALU.logical_shift_right))
                link(dve.tensor_scalar(pos_u[:, 1, :, :, :], where, 7, None, ALU.bitwise_and))
                row, place = (pos_u[:, c, :, :, :].rearrange("p s h g -> p (s h g)") for c in range(2))
                a_of, b_of, add = (pos_b[:, c, :, :, :].rearrange("p s h g -> p (s h g)") for c in range(3))
                mark(dve.tensor_scalar(a_of, row, -1.0, 0.0, ALU.add, ALU.max))
                link(dve.tensor_scalar(add, row, 1.0, 8.0, ALU.is_equal, ALU.mult))
                link(dve.tensor_tensor(b_of, place, add, ALU.add))
                slots = HALVES * GROUP * TOPK
                link(dve.tensor_tensor(match[:, :, :, :],
                                       pos_b[:, 0:2, :, :, :].rearrange("p a s h g -> p a (s h g)").unsqueeze(2)
                                       .to_broadcast([P, 2, TOPK, slots]),
                                       iota16[:, :, :].unsqueeze(1).to_broadcast([P, 2, TOPK, slots]), ALU.is_equal))
                hg = HALVES * GROUP
                ranks = match[:, :, :, :].rearrange("p a k (s c) -> p (a k) s c", c=hg)
                link(dve.tensor_tensor(ranks, ranks, key_idb[:, :, :, :, :].rearrange("p a k h g -> p (a k) (h g)")
                                       .unsqueeze(2).to_broadcast([P, 2 * TOPK, TOPK, hg]), ALU.mult))
                n = TOPK // 2
                while n > 1:
                    link(dve.tensor_tensor(match[:, :, 0:n, :], match[:, :, 0:n, :], match[:, :, n:2 * n, :], ALU.add))
                    n //= 2
                for a in range(2):
                    lo, hi = (match[:, a, k, :].rearrange("p (s h g) -> p s h g", h=HALVES, g=GROUP) for k in range(2))
                    for h in range(HALVES):
                        last = mark(dve.tensor_tensor(chosen[:, h, a, GROUP * TOPK * q:GROUP * TOPK * (q + 1)]
                                                      .rearrange("p (g s) -> p s g", s=TOPK), lo[:, :, h, :], hi[:, :, h, :],
                                                      ALU.add))
                dve.wait_ge(dve_step, last)

            dve.wait_ge(iota_ready, 2)
            for hp in range(HP):
                top_keys(hp)
                if hp % 2:
                    top_candidates(hp // 2)
                if hp == 2 * GROUP - 1:
                    resolve(0)
            wide = [P, HALVES, PEER_HEADS, TOPK]
            dve.tensor_tensor(gexp[:, :, :, :], best[:, :, :, :], best[:, :, :, 0:1].to_broadcast(wide), ALU.subtract)\
               .then_inc(gexp_in, 1)
            resolve(1)
            dve.wait_ge(gexp_done, 1)
            link(dve.tensor_reduce(gsum[:, 0, :, :], gexp[:, :, :, :], AX.X, ALU.add))
            link(dve.reciprocal(gsum[:, 1, :, :], gsum[:, 0, :, :]))
            for h in range(HALVES):
                dve.tensor_tensor(chosen[:, h, 2, :].rearrange("p (h k) -> p h k", k=TOPK), gexp[:, h, :, :],
                                  gsum[:, 1, h, :].unsqueeze(2).to_broadcast([P, PEER_HEADS, TOPK]), ALU.mult)\
                   .then_inc(chosen_ready, 1)

            def ut_rest_half(t, p, b):
                need(dve, ut_hi_done, 2 * t + (b + 1))
                if b == 0:
                    need(dve, h_done, t - 1)
                dve.tensor_tensor(ut_lo[:, p, 4 * b:4 * b + 4, :].rearrange("p a b -> p (a b)"), ps[b][:, :],
                                  ut_hi[:, p, 4 * b:4 * b + 4, :].rearrange("p a b -> p (a b)").bitcast(F32),
                                  ALU.subtract).then_inc(ut_lo_done, 1)

            def ut_rest(t, p):
                ut_rest_half(t, p, 0)
                ut_rest_half(t, p, 1)

            ut_rest(TAIL_TILES, TAIL_TILES % 2)
            dve.wait_ge(routesT_done, 1)
            mark(dve.tensor_copy(routes[:, 0:2, :].rearrange("p a t -> p (a t)"), ps[3][:, :]))
            gate_in = ps[2][:, SEQ:2 * SEQ]
            link(dve.tensor_copy(routes[:, 2, :], gate_in))
            link(dve.tensor_tensor(rest[:, 0, :], gate_in, routes[:, 2, :], ALU.subtract))
            link(dve.tensor_copy(routes[:, 3, :], rest[:, 0, :]))
            link(dve.tensor_tensor(rest[:, 1, :], rest[:, 0, :], routes[:, 3, :], ALU.subtract))
            dve.tensor_copy(routes[:, 4, :], rest[:, 1, :]).then_inc(routes_ready, 1)
            dve.wait_ge(routes_ready, 1)

            def hot_rows(i, b, first):
                if not first:
                    dve.wait_ge(gate_done, 4 * i + (2 * b - 2))
                cols = bass.ds(i * 16 + b * TOK_STEP, TOK_STEP)

                def rows(a, n):
                    return routes[:, a:a + n, cols].unsqueeze(2).to_broadcast([P, n, N_KEYS, TOK_STEP])

                dve.tensor_tensor(hot[:, b, :, :, :], key_no[:, :, :].unsqueeze(1).to_broadcast([P, 2, N_KEYS, TOK_STEP]),
                                  rows(0, 2), ALU.is_equal).then_inc(hot_ready, 1)
                dve.wait_ge(hot_ready, 4 * i + (2 * b + 1))
                dve.tensor_tensor(gated1[:, b, :, :, :],
                                  hot[:, b, 0, :, :].unsqueeze(1).to_broadcast([P, 3, N_KEYS, TOK_STEP]),
                                  rows(2, 3), ALU.mult).then_inc(hot_ready, 1)

            def gate_step(i, p, first):
                for b in range(2):
                    hot_rows(i, b, first)
                    ut_rest_half(i + (TAIL_TILES + 1), 1 - p, b)

            gate_step(0, 0, True)
            gate_step(1, 1, False)
            with dve.Fori(0, GATE_TILES // 2 - 1) as turn:
                for p in range(2):
                    gate_step(turn * 2 + (2 + p), p, False)

            def gated(t, p):
                need(dve, h_loaded[p], (t - p) * 8 + 16)
                dve.tensor_tensor(h_in[:, p, :], h_in[:, p, :],
                                  gate_m[:, :, bass.ds(t, 1)].rearrange("p c a -> p (c a)"), ALU.mult).then_inc(act_done, 1)

            def v_rest(t, p):
                need(dve, act_hi_done, t + 1)
                need(dve, v_used, t - 1)
                dve.tensor_tensor(act_lo[:, p, :], h_in[:, p, :], act_hi[:, p, :].bitcast(F32), ALU.subtract)\
                   .then_inc(act_lo_done, 1)
                need(dve, v_hi_done, t + 1)
                dve.tensor_tensor(v_lo[:, p, :], v_raw[:, p, :], v_hi[:, p, :].bitcast(F32), ALU.subtract)\
                   .then_inc(v_lo_done, 1)

            dve.wait_ge(gate_ready, SEQ // 4)
            gated(0, 0)
            v_rest(0, 0)
            with dve.Fori(0, (TILES - LAG - 2) // 2) as turn:
                for p in range(2):
                    s = turn * 2 + (LAG + p)
                    gated(s - (LAG - 1), 1 - p)
                    ut_rest(s + 1, 1 - p)
                    v_rest(s - (LAG - 1), 1 - p)
            for s in range(TILES - 2, TILES):
                gated(s - (LAG - 1), (s + 1) % 2)
                if s + 1 < TILES:
                    ut_rest(s + 1, (s + 1) % 2)
                v_rest(s - (LAG - 1), (s + 1) % 2)
            with dve.Fori(0, (LAG - 2) // 2) as turn:
                for p in range(2):
                    gated(turn * 2 + (TILES - LAG + 1 + p), 1 - p)
                    v_rest(turn * 2 + (TILES - LAG + 1 + p), 1 - p)
            gated(TILES - 1, 1)
            v_rest(TILES - 1, 1)
            dve.wait_ge(v_used, TILES)
            for c in range(2):
                dve.tensor_copy(gate_m[:, 8 + 4 * c:12 + 4 * c, :].rearrange("p a b -> p (a b)"), ps[6 + c][:, :])\
                   .then_inc(y_ready, 1)

        @block.tensor
        def _(pe):
            mm = pe.matmul
            pe.wait_ge(ident_ready, 1)
            pe.wait_ge(gains_loaded, 16 * 7)
            pe.transpose(ps[5][:, 0:N_GAINS], gain_rows[:, :], ident[0:N_GAINS, 0:N_GAINS]).then_inc(gainsT_done, 1)

            def feat_transposes(rnd, first_bank, src_sem, base_count):
                for pair in range(4):
                    if pair >= 2:
                        pe.wait_ge(feat_ready, rnd * 4 + pair - 1)
                    for i in range(2):
                        k = 2 * pair + i
                        for h in range(HALVES):
                            ins = pe.transpose(ps[first_bank + pair % 2][:, i * SEQ + h * P:i * SEQ + (h + 1) * P],
                                               scaled[:, h, k * P:(k + 1) * P], ident[:, :])
                    ins.then_inc(feat_done, 1)

            pe.wait_ge(scaled_ready, 2)
            feat_transposes(0, 6, None, None)
            pe.wait_ge(feat_ready, 4)

            def qk_transposes(g):
                pe.wait_ge(normed_ready, g + 1)
                if g >= 2:
                    pe.wait_ge(qkT_ready, g - 1)
                for b in range(4):
                    ins = pe.transpose(ps[4 + g % 2][:, b * P:(b + 1) * P], normed[:, g % 2, b * P:(b + 1) * P], ident[:, :])
                ins.then_inc(qkT_done, 1)

            pe.wait_ge(gains_ready, 1)
            for g in range(GROUPS):
                w, h = divmod(g, HALVES)
                if h == 0:
                    pe.wait_ge(w_loaded[w % W_SLOTS], 16 * (w // W_SLOTS + 1))
                if 4 <= g < QK_GROUPS + 4:
                    pe.wait_ge(normed_ready, g - 3)
                for k in range(KD):
                    ins = mm(ps[g % 4][:, :], featT[:, k, h * P:(h + 1) * P], w_ring[:, w % W_SLOTS, k, :],
                             start=k == 0, stop=k == KD - 1)
                ins.then_inc(proj_done, 1)
                if h == 1:
                    pe.wait_ge(proj_done, g + 1)
                    pe.sem_inc(w_used, 1)
                if 1 <= g <= QK_GROUPS:
                    qk_transposes(g - 1)
            pe.wait_ge(sk_loaded, 16)
            for j in range(4):
                pe.wait_ge(qkT_ready, QK_GROUPS)
                if j >= 2:
                    pe.wait_ge(skT_ready, j - 1)
                for i in range(4):
                    ins = pe.transpose(ps[4 + j % 2][:, i * P:(i + 1) * P], sk_nat[:, 4 * j + i, :], ident[:, :])
                ins.then_inc(skT_done, 1)
            pe.wait_ge(values_ready, 4)
            pe.wait_ge(skT_ready, 4)

            def logits_of(n):
                q, k, b, r, _ = instance(n)
                if n >= 2:
                    pe.wait_ge(nmax_ready, n - 1)
                rows = slice(r, r + HEAD)
                mm(ps[n % 2][:, 0:P], qkT[rows, q, b, 0:P], qkT[rows, k, b, 0:P], start=True, stop=True)
                mm(ps[n % 2][:, P:3 * P], qkT[rows, q, b, P:SEQ], qkT[rows, k, b, :], start=True, stop=True)\
                    .then_inc(logits_done, 1)

            def probs_transposes(m):
                if m < MOBA_HEADS:
                    src = expd[:, m % 4, :]
                    pe.wait_ge(exp_done, m + 1)
                else:
                    src = mixed[:, m % 2, :]
                    pe.wait_ge(mixed_ready, m - MOBA_HEADS + 1)
                if m >= 2:
                    pe.wait_ge(probsT_ready, m - 1)
                for i in range(3):
                    ins = pe.transpose(ps[2 + m % 2][:, i * P:(i + 1) * P], src[:, i * P:(i + 1) * P], ident[:, :])
                ins.then_inc(probsT_done, 1)

            def values_of(m):
                pe.wait_ge(probsT_ready, m + 1)
                if m < MOBA_HEADS:
                    kind, bank, cols = 0, 4, slice(m * HEAD, (m + 1) * HEAD)
                else:
                    kind, bank, cols = 1, 6, slice((m - MOBA_HEADS) * P, (m - MOBA_HEADS + 1) * P)
                pT = probsT[:, m % 2, :]
                mm(ps[bank][:, cols], pT[:, 0:P], v_sb[:, kind, 0, cols], start=True, stop=True)
                mm(ps[bank + 1][:, cols], pT[:, P:2 * P], v_sb[:, kind, 0, cols], start=True, stop=False)
                mm(ps[bank + 1][:, cols], pT[:, 2 * P:3 * P], v_sb[:, kind, 1, cols], start=False, stop=True)\
                    .then_inc(heads_done, 1)

            n = 0
            for m in range(MIXES):
                while n < min(exps_for(m) + 2, INSTANCES):
                    logits_of(n)
                    n += 1
                probs_transposes(m)
                if m:
                    values_of(m - 1)
            values_of(MIXES - 1)

            pe.wait_ge(mix_ready, 4)
            feat_transposes(1, 0, None, None)
            pe.wait_ge(feat_ready, 8)
            for c in range(2):
                w = 6 + c
                pe.wait_ge(w_loaded[w % W_SLOTS], 16 * (w // W_SLOTS + 1))
                for h in range(HALVES):
                    y = ps[4 + 2 * h + c]
                    for k in range(KD):
                        mm(y[:, :], featT[:, k, h * P:(h + 1) * P], w_ring[:, w % W_SLOTS, k, :], start=k == 0, stop=False)
                    ins = mm(y[:, :], ident[:, :], x_sb[:, h, c * COLS:(c + 1) * COLS], start=False, stop=True)
                ins.then_inc(x2_done, 1)
                pe.wait_ge(x2_done, c + 1)
                pe.sem_inc(w_used, 1)
            pe.wait_ge(scaled_ready, 2 + 4)
            feat_transposes(2, 0, None, None)
            pe.wait_ge(feat_ready, 12)

            def key_scores(hp):
                pe.wait_ge(query_ready, hp + 1)
                if hp >= 2:
                    pe.wait_ge(scores_ready, hp - 1)
                for h in range(HALVES):
                    ins = mm(ps[hp % 2][:, h * P:(h + 1) * P], qT[:, hp % 2, h * P:(h + 1) * P], skT[:, hp, :],
                             start=True, stop=True)
                ins.then_inc(scores_done, 1)

            for hp in range(HP):
                w, c = 8 + hp // 4, hp % 4
                if c == 0:
                    pe.wait_ge(w_loaded[w % W_SLOTS], 16 * (w // W_SLOTS + 1))
                if hp >= 2:
                    pe.wait_ge(query_ready, hp - 1)
                for k in range(KD):
                    ins = mm(ps[2 + hp % 2][:, 0:SEQ], w_ring[:, w % W_SLOTS, k, c * P:(c + 1) * P], featT[:, k, :],
                             start=k == 0, stop=k == KD - 1)
                ins.then_inc(query_done, 1)
                if c == 3:
                    pe.wait_ge(query_done, hp + 1)
                    pe.sem_inc(w_used, 1)
                if hp:
                    key_scores(hp - 1)
            key_scores(HP - 1)
            def transposes(t, p, halves=(0, 1), plain=False):
                if 0 in halves:
                    need(pe, u_loaded[p], (t - p) * 8 + 16)
                for b in halves:
                    if plain:
                        need(pe, ut_hi_done, 2 * t + (b - 1))
                    else:
                        need(pe, ut_lo_done, 2 * t + (b - 1 - 2 * TAIL_TILES))
                    for i in range(4):
                        k = 4 * b + i
                        ins = pe.transpose(ps[b][:, i * P:(i + 1) * P], u_raw[:, p, k * P:(k + 1) * P], ident[:, :])
                    ins.then_inc(ut_done, 1)

            def x_dot_u(t, p, bank, ks):
                for k in ks:
                    for n, (a, b) in enumerate(((ut_hi, xn_hi), (ut_hi, xn_lo), (ut_lo, xn_hi))):
                        ins = mm(ps[bank][:, 0:SEQ], a[:, p, k, :], b[:, k, :], start=k == 0 and n == 0,
                                 stop=k == KD - 1 and n == 2)
                if KD - 1 in ks:
                    ins.then_inc(h_done, 1)

            def times_v(t, p):
                need(pe, act_lo_done, t + 1)
                need(pe, v_lo_done, t + 1)
                for h in range(HALVES):
                    for a, b in ((act_hi, v_hi), (act_hi, v_lo), (act_lo, v_hi)):
                        for c in range(2):
                            ins = mm(ps[4 + 2 * h + c][:, :], a[:, p, h * P:(h + 1) * P], b[:, p, c * COLS:(c + 1) * COLS],
                                     start=False, stop=True, skip_group_check=True)
                ins.then_inc(v_used, 1)

            pe.wait_ge(xn_lo_done, 4)
            pe.wait_ge(scores_ready, HP)
            transposes(0, 0, plain=True)
            for s in range(TAIL_TILES):
                transposes(s + 1, (s + 1) % 2, plain=True)
                need(pe, ut_hi_done, 2 * s + 2)
                need(pe, gelu_done, s)
                for k in range(KD):
                    ins = mm(ps[2][:, 0:SEQ], ut_plain[:, s % 2, k, :], featT[:, k, :], start=k == 0,
                             stop=k == KD - 1)
                ins.then_inc(h_done, 1)
            pe.wait_ge(chosen_ready, HALVES)
            pe.wait_ge(gelu_done, TAIL_TILES)
            for h in range(HALVES):
                for a in range(2):
                    pe.transpose(ps[3][:, a * SEQ + h * P:a * SEQ + (h + 1) * P], chosen[:, h, a, :], ident[:, :])
                ins = pe.transpose(ps[2][:, SEQ + h * P:SEQ + (h + 1) * P], chosen[:, h, 2, :], ident[:, :])
            ins.then_inc(routesT_done, 1)

            def gate_tokens(i, n, first=False):
                b = n // 2
                if n % 2 == 0:
                    pe.wait_ge(hot_ready, 4 * i + (2 * b + 2))
                if not first:
                    pe.wait_ge(gate_ready, 4 * i + n)
                for j in range(4):
                    tok = 4 * (n % 2) + j
                    for a in range(3):
                        ins = mm(ps[3][:, j * P:(j + 1) * P], hot[:, b, 1, :, tok], gated1[:, b, a, :, tok],
                                 start=a == 0, stop=a == 2)
                ins.then_inc(gate_done, 1)

            def gate_step(i, p, first):
                t = i + TAIL_TILES
                pe.wait_ge(ut_lo_done, i * 2 + 2)
                need(pe, gelu_done, t)
                if first:
                    pe.wait_ge(routes_ready, 1)
                x_dot_u(t, p, 2, range(0, 2))
                if not first:
                    gate_tokens(i - 1, 2)
                transposes(t + 1, 1 - p, [0])
                x_dot_u(t, p, 2, range(2, 4))
                if not first:
                    gate_tokens(i - 1, 3)
                transposes(t + 1, 1 - p, [1])
                x_dot_u(t, p, 2, range(4, 6))
                gate_tokens(i, 0, first)
                x_dot_u(t, p, 2, range(6, 8))
                gate_tokens(i, 1)

            gate_step(0, 0, True)
            gate_step(1, 1, False)
            with pe.Fori(0, GATE_TILES // 2 - 1) as turn:
                for p in range(2):
                    gate_step(turn * 2 + (2 + p), p, False)

            gate_tokens(GATE_TILES - 1, 2)
            gate_tokens(GATE_TILES - 1, 3)
            pe.wait_ge(gate_ready, SEQ // 4)
            pe.wait_ge(gelu_done, LAG)

            def full_step(s, p, last=False):
                if not last:
                    transposes(s + 1, 1 - p)
                need(pe, ut_lo_done, 2 * s + (2 - 2 * TAIL_TILES))
                need(pe, gelu_done, s - 1)
                x_dot_u(s, p, 2 + p, range(KD))
                times_v(s - LAG, p)

            with pe.Fori(0, (TILES - LAG - 2) // 2) as turn:
                for p in range(2):
                    full_step(turn * 2 + (LAG + p), p)
            full_step(TILES - 2, 0)
            full_step(TILES - 1, 1, last=True)
            with pe.Fori(0, LAG // 2) as turn:
                for p in range(2):
                    times_v(turn * 2 + (TILES - LAG + p), p)


_INS = ['x', 'norm1_g', 'w_in', 'moba_qk_norm_g', 'diff_qk_norm_g', 'diff_lambda', 'diff_subln_g', 'w_out', 'norm2_g',
        'peer_w_query', 'peer_sub_keys', 'peer_u', 'peer_v']


def kernel(**inputs):
    import numpy as _np
    import concourse.bacc as _bacc
    from concourse import mybir as _mybir
    from concourse.bass_utils import run_bass_kernel_spmd as _run

    nc = _bacc.Bacc("TRN2", target_bir_lowering=False, num_devices=1)
    arrays, args = {}, []
    for name in _INS:
        a = _np.ascontiguousarray(inputs[name])
        arrays[f"in_{name}_dram"] = a
        args.append(nc.dram_tensor(f"in_{name}_dram", a.shape, _mybir.dt.from_np(a.dtype), kind="ExternalInput").ap())
    args.append(nc.dram_tensor("out_0_dram", (1, SEQ, D), _mybir.dt.float32, kind="ExternalOutput").ap())
    layer(nc, *args)
    r = _run(nc, [arrays], core_ids=[0])
    return r.results[0]["out_0_dram"]
```

```python
import math
from contextlib import ExitStack

import concourse.bass as bass
from concourse import mybir

F32 = mybir.dt.float32
F32R = mybir.dt.float32r
U32 = mybir.dt.uint32
BF16 = mybir.dt.bfloat16
ALU = mybir.AluOpType
ACT = mybir.ActivationFunctionType
AX = mybir.AxisListType

P = 128
SEQ = 256
D = 1024
HALVES = SEQ // P
KD = D // P
HEAD = 64
MOBA_HEADS = 8
DIFF_HEADS = 4
COLS = 512
TOPK = 16
PEER_HEADS = 8
N_KEYS = 128
SLOTS = PEER_HEADS * TOPK
HP = PEER_HEADS * 2
TILES = N_KEYS
EPS = 1e-6
LAM_INIT = 0.8 - 0.6 * math.exp(-0.3 * 0)
MASKED = -1.0e30
REMOVED = -3.0e38
W_LOADS = 4
W_PARTS = 3
CHUNK = 4 * COLS
PROJ_CHUNKS = 12
W_CHUNKS = PROJ_CHUNKS + 4 + 8
TAIL_TILES = 4
GATE_TILES = 16
LAG = TAIL_TILES + GATE_TILES
assert LAG % 4 == 0 and TILES % 4 == 0
CAND_ROWS = 17
BLOCK_ORDER = [3, 4, 5, 0, 1, 2]
QK_TURN = {0: 0, 1: 1, 3: 2, 4: 3}
QK_TENSOR = [2, 3, 0, 1]
INSTANCES = MOBA_HEADS + 2 * DIFF_HEADS
TOK_STEP = 8
GROUP = 2
G1, G2, GQK, GSUB = 0, 8, 16, 20
N_GAINS = 21


def layer(nc, x, norm1_g, w_in, moba_g, diff_g, diff_lambda, subln_g, w_out, norm2_g, w_query, sub_keys,
          peer_u, peer_v, out):
    keep = ExitStack()

    base = (nc.sbuf_base + 31) // 32 * 32

    class Region:
        def __init__(self, at):
            self.at = at

        def put(self, name, shape, dt=F32):
            t = nc.alloc_sbuf_tensor_at(name, shape, dt, offset=self.at)
            size = 2 if dt == BF16 else 4
            for n in shape[1:]:
                size *= n
            self.at += (size + 31) // 32 * 32
            return t

    whole = Region(base)
    ident = whole.put("ident", [P, P])
    gains = whole.put("gains", [P, N_GAINS])
    routes = whole.put("routes", [P, 5, SEQ], BF16)
    xn_hi = whole.put("xn_hi", [P, KD, SEQ], F32R)
    xn_lo = whole.put("xn_lo", [P, KD, SEQ], F32R)
    stream_at = whole.at
    u_raw = whole.put("u_raw", [P, 2, D])
    v_raw = whole.put("v_raw", [P, 2, D])
    ut_hi_at = whole.at
    ut_hi = whole.put("ut_hi", [P, 2, KD, P], F32R)
    ut_lo = whole.put("ut_lo", [P, 2, KD, P], F32R)
    h_out = whole.put("h_out", [P, 2, SEQ])
    h_in = whole.put("h_in", [P, 2, SEQ])
    split_at = whole.at
    act_hi = whole.put("act_hi", [P, 2, SEQ], F32R)
    act_lo = whole.put("act_lo", [P, 2, SEQ], F32R)
    v_hi = whole.put("v_hi", [P, 2, D], F32R)
    v_lo = whole.put("v_lo", [P, 2, D], F32R)
    whole.at += 2048
    arena_at = whole.at
    gate_m = whole.put("gate_m", [P, SEQ, N_KEYS])

    over = Region(split_at)
    hot = over.put("hot", [P, 2, 2, N_KEYS, TOK_STEP], BF16)
    gated1 = over.put("gated1", [P, 2, 3, N_KEYS, TOK_STEP], BF16)
    key_no = over.put("key_no", [P, N_KEYS, TOK_STEP], BF16)
    assert over.at <= arena_at
    over = Region(ut_hi_at)
    ut_plain = over.put("ut_plain", [P, 2, KD, P])
    over = Region(split_at)
    qT = over.put("qT", [P, 2, SEQ])

    over = Region(arena_at)
    w_raw = over.put("w_raw", [P, W_LOADS, CHUNK])
    w_hi = over.put("w_hi", [P, W_PARTS, 4, COLS], F32R)
    under_feat = Region(over.at)
    qk_raw = under_feat.put("qk_raw", [P, HALVES, COLS])
    squares = under_feat.put("squares", [P, 2, COLS])
    featT = over.put("featT", [P, KD, SEQ])
    skT = over.put("skT", [P, HP, N_KEYS])
    routing_at = over.at
    bias_t = over.put("bias_t", [P, MOBA_HEADS, 3 * P])
    v_sb = over.put("v_sb", [P, 2, HALVES, COLS])
    x_sb = over.put("x_sb", [P, HALVES, D])
    scaled = over.put("scaled", [P, HALVES, D])
    gain_rows = over.put("gain_rows", [N_GAINS, P])
    sk_nat = over.put("sk_nat", [P, HP, P])
    logits = over.put("logits", [P, 2, 3 * P])
    probsT = over.put("probsT", [P, 2, 3 * P])
    lam_in = over.put("lam_in", [P, 4 * HEAD])
    lam_prod = over.put("lam_prod", [P, 2, HEAD])
    tiny = {}
    for name, n in (("ssq", 2), ("ms", 2), ("sd", 2), ("rstd", 2), ("dots", 2), ("edots", 2), ("lam", 2),
                    ("qk_ss", 64), ("qk_ms", 64), ("qk_sd", 64), ("qk_rs", 64), ("nmax", 32), ("sums", 32),
                    ("rsum", 32), ("rlam", 8), ("d_ss", 8), ("d_ms", 8), ("d_sd", 8), ("d_rs", 8),
                    ("ssq2", 4), ("ms2", 2), ("sd2", 2), ("rstd2", 2), ("ssq2s", 2), ("unused", 2)):
        tiny[name] = over.put("t_" + name, [P, n])
    assert over.at <= arena_at + 4 * SEQ * N_KEYS

    over = Region(stream_at)
    qkT = over.put("qkT", [P, 4, 4, SEQ])
    normed = over.put("normed", [P, 2, COLS])
    expd = over.put("expd", [P, 4, 3 * P])
    mixed = over.put("mixed", [P, 2, 3 * P])
    w_lo = over.put("w_lo", [P, W_PARTS, 4, COLS], F32R)
    assert over.at <= arena_at
    over = Region(routing_at)
    scores = over.put("scores", [P, HALVES, HP, N_KEYS])
    key_val = over.put("key_val", [P, HALVES, HP, TOPK])
    key_idx = over.put("key_idx", [P, HALVES, HP, TOPK], U32)
    cand = over.put("cand", [P, 2, HALVES, CAND_ROWS * 8])
    best = over.put("best", [P, HALVES, PEER_HEADS, TOPK])
    pos = over.put("pos", [P, HALVES, PEER_HEADS, TOPK], U32)
    key_idb = over.put("key_idb", [P, 2, 2, TOPK, HALVES, GROUP], BF16)
    pos_u = over.put("pos_u", [P, 2, TOPK, HALVES, GROUP], U32)
    pos_b = over.put("pos_b", [P, 3, TOPK, HALVES, GROUP], BF16)
    match = over.put("match", [P, 2, 2, TOPK, HALVES * GROUP * TOPK], BF16)
    iota16 = over.put("iota16", [P, TOPK, HALVES * GROUP * TOPK], BF16)
    chosen = over.put("chosen", [P, HALVES, 3, SLOTS])
    gexp = over.put("gexp", [P, HALVES, PEER_HEADS, TOPK])
    gsum = over.put("gsum", [P, 2, HALVES, PEER_HEADS])
    rest = over.put("rest", [P, 2, SEQ])
    assert over.at <= arena_at + 4 * SEQ * N_KEYS

    with keep:
        h_spill = nc.dram_tensor("h_spill", (TILES, P, SEQ), F32, kind="Internal").ap()
        ps = [keep.enter_context(nc.psum_tensor(f"bank{i}", [P, COLS], F32)) for i in range(8)]

        def sem(name):
            return keep.enter_context(nc.semaphore(name))

        x_loaded = [sem(f"x_loaded{h}") for h in range(HALVES)]
        gains_loaded = sem("gains_loaded")
        lam_loaded = sem("lam_loaded")
        sk_loaded = sem("sk_loaded")
        w_loaded = [sem(f"w_loaded{i}") for i in range(W_LOADS)]
        u_loaded = [sem(f"u_loaded{i}") for i in range(2)]
        v_loaded = [sem(f"v_loaded{i}") for i in range(2)]
        vx_loaded = [sem(f"vx_loaded{i}") for i in range(2)]
        h_stored = [sem(f"h_stored{i}") for i in range(2)]
        h_loaded = [sem(f"h_loaded{i}") for i in range(2)]
        stored = sem("stored")
        ident_ready = sem("ident_ready")
        pool_step = sem("pool_step")
        bias_ready = sem("bias_ready")
        iota_ready = sem("iota_ready")
        dve_step = sem("dve_step")
        gainsT_done = sem("gainsT_done")
        gains_ready = sem("gains_ready")
        ssq_done = sem("ssq_done")
        ms_ready = sem("ms_ready")
        sd_ready = sem("sd_ready")
        scaled_ready = sem("scaled_ready")
        feat_done = sem("feat_done")
        feat_ready = [sem("feat_ready_even"), sem("feat_ready_odd")]
        w_hi_done = sem("w_hi_done")
        w_lo_done = sem("w_lo_done")
        proj_done = sem("proj_done")
        w_used = sem("w_used")
        copied = sem("copied")
        sq_done = sem("sq_done")
        qk_ms_ready = sem("qk_ms_ready")
        qk_sd_ready = sem("qk_sd_ready")
        qk_rs_ready = sem("qk_rs_ready")
        normed_ready = sem("normed_ready")
        qkT_done = sem("qkT_done")
        qkT_ready = sem("qkT_ready")
        skT_done = sem("skT_done")
        skT_ready = sem("skT_ready")
        d_logits_done = sem("d_logits_done")
        d_nmax_ready = sem("d_nmax_ready")
        d_exp_done = sem("d_exp_done")
        mixed_ready = sem("mixed_ready")
        d_probsT_done = sem("d_probsT_done")
        d_probsT_ready = sem("d_probsT_ready")
        d_heads_done = sem("d_heads_done")
        d_mix_ready = sem("d_mix_ready")
        logits_done = sem("logits_done")
        nmax_ready = sem("nmax_ready")
        exp_done = sem("exp_done")
        probsT_done = sem("probsT_done")
        probsT_ready = sem("probsT_ready")
        heads_done = sem("heads_done")
        dots_ready = sem("dots_ready")
        edots_ready = sem("edots_ready")
        d_sq_done = sem("d_sq_done")
        d_ms_ready = sem("d_ms_ready")
        d_sd_ready = sem("d_sd_ready")
        mix_ready = sem("mix_ready")
        x2_done = sem("x2_done")
        rstd2_ready = sem("rstd2_ready")
        x2_scaled = sem("x2_scaled")
        xn_hi_done = sem("xn_hi_done")
        xn_lo_done = sem("xn_lo_done")
        query_done = sem("query_done")
        query_ready = sem("query_ready")
        scores_done = sem("scores_done")
        scores_ready = sem("scores_ready")
        places_ready = sem("places_ready")
        resolved = sem("resolved")
        pool_link = sem("pool_link")
        chosen_ready = sem("chosen_ready")
        routesT_done = sem("routesT_done")
        gates_read = sem("gates_read")
        routes_ready = sem("routes_ready")
        gexp_in = sem("gexp_in")
        gexp_done = sem("gexp_done")
        hot_ready = sem("hot_ready")
        gate_done = sem("gate_done")
        gate_ready = sem("gate_ready")
        ut_done = sem("ut_done")
        ut_hi_done = sem("ut_hi_done")
        ut_lo_done = sem("ut_lo_done")
        h_done = sem("h_done")
        gelu_done = sem("gelu_done")
        act_done = sem("act_done")
        act_hi_done = sem("act_hi_done")
        act_lo_done = sem("act_lo_done")
        v_hi_done = sem("v_hi_done")
        v_lo_done = sem("v_lo_done")
        v_used = sem("v_used")
        y_half_done = sem("y_half_done")
        y_ready = [sem(f"y_ready{h}") for h in range(HALVES)]

        def need(eng, s, value):
            if not isinstance(value, int) or value > 0:
                eng.wait_ge(s, value)

        def w_source(j):
            if j >= PROJ_CHUNKS + 4:
                c = j - PROJ_CHUNKS - 4
                return w_query[0, :, c * 256:(c + 1) * 256].rearrange("(k p) n -> p k n", p=P)
            w, kh = divmod(j, 2)
            m, c = (w_in, BLOCK_ORDER[w]) if w < 6 else (w_out, w - 6)
            if w >= 6:
                kh = 1 - kh
            return m[0, kh * COLS:(kh + 1) * COLS, c * COLS:(c + 1) * COLS].rearrange("(k p) n -> p k n", p=P)

        def instance(n):
            if n < MOBA_HEADS:
                return 0, 1, n // 2, HEAD * (n % 2), n
            i, j = divmod(n - MOBA_HEADS, 2)
            return 2, 3, i, HEAD * j, 2 * i + 1

        def normalise(eng, q):
            eng.tensor_tensor(normed[:, q % 2, :].rearrange("p (h d) -> p h d", d=HEAD),
                              qk_raw[:, q % 2, :].rearrange("p (h d) -> p h d", d=HEAD),
                              tiny["qk_rs"][:, 8 * q:8 * q + 8].unsqueeze(2).to_broadcast([P, 8, HEAD]), ALU.mult)\
               .then_inc(normed_ready, 1)

        def resolve(eng, link, q):
            hg = HALVES * GROUP
            m = match[:, q % 2, :, :, :]
            ranks = m.rearrange("p a k (s c) -> p (a k) s c", c=hg)
            link(eng.tensor_tensor(ranks, ranks, key_idb[:, q % 2, :, :, :, :].rearrange("p a k h g -> p (a k) (h g)")
                                   .unsqueeze(2).to_broadcast([P, 2 * TOPK, TOPK, hg]), ALU.mult))
            n = TOPK // 2
            while n > 1:
                link(eng.tensor_tensor(m[:, :, 0:n, :], m[:, :, 0:n, :], m[:, :, n:2 * n, :], ALU.add))
                n //= 2
            for a in range(2):
                lo, hi = (m[:, a, k, :].rearrange("p (s h g) -> p s h g", h=HALVES, g=GROUP) for k in range(2))
                for h in range(HALVES):
                    link(eng.tensor_tensor(chosen[:, h, a, GROUP * TOPK * q:GROUP * TOPK * (q + 1)]
                                           .rearrange("p (g s) -> p s g", s=TOPK), lo[:, :, h, :], hi[:, :, h, :], ALU.add))

        def group_bank(w, h):
            return h + 2 if w == 0 else h

        def tail_bank(s):
            return 2 if s == TAIL_TILES - 1 else 2 + s % 2

        first_v = TILES - LAG

        def v_slot(q):
            if q < 2:
                return v_raw[:, q, :], v_hi[:, q, :], v_lo[:, q, :]
            return (u_raw[:, q - 2, :], ut_hi[:, q - 2, :, :].rearrange("p k n -> p (k n)"),
                    ut_lo[:, q - 2, :, :].rearrange("p k n -> p (k n)"))

        def v_arrival(q, e4):
            if q < 2:
                return v_loaded[q], e4 * 16 + (first_v // 2 * 16 + 16)
            return vx_loaded[q - 2], e4 * 16 + 16

        block = keep.enter_context(nc.Block())

        @block.sync
        def _(sp):
            for h in range(HALVES):
                sp.dma_start(x_sb[:, h, :], x[0, h * P:(h + 1) * P, :]).then_inc(x_loaded[h], 16)
            for j in range(W_CHUNKS):
                if j >= W_LOADS:
                    sp.wait_ge(w_lo_done if j - W_LOADS < PROJ_CHUNKS + 4 else w_used, j - W_LOADS + 1)
                n = 4 if j < PROJ_CHUNKS + 4 else KD
                sp.dma_start(w_raw[:, j % W_LOADS, :].rearrange("p (k n) -> p k n", k=n), w_source(j))\
                  .then_inc(w_loaded[j % W_LOADS], 16)
                if j == 0:
                    rows = [(G1, KD, norm1_g[0].rearrange("(r c) -> r c", c=P)),
                            (G2, KD, norm2_g[0].rearrange("(r c) -> r c", c=P)), (GSUB, 1, subln_g)]
                    for r, n, src in rows:
                        sp.dma_start(gain_rows[r:r + n, :], src).then_inc(gains_loaded, 16)
                    for r, src in ((GQK, moba_g[0]), (GQK + 2, diff_g[0])):
                        for c in range(2):
                            sp.dma_start(gain_rows[r:r + 2, c * HEAD:(c + 1) * HEAD], src).then_inc(gains_loaded, 16)
                    sp.dma_start(lam_in[:, :], diff_lambda.rearrange("a b c -> a (b c)").to_broadcast([P, 4 * HEAD]))\
                      .then_inc(lam_loaded, 16)
                if j == 5:
                    sp.dma_start(sk_nat[:, :, :], sub_keys[0].rearrange("h a n d -> n (h a) d")).then_inc(sk_loaded, 16)

            def load_u(t, p, held=True):
                if held:
                    sp.wait_ge(ut_done, 2 * t - 2)
                sp.dma_start(u_raw[:, p, :], peer_u[0, bass.ds(t * P, P), :]).then_inc(u_loaded[p], 16)

            def load_v(t, p, held=True):
                if held:
                    sp.wait_ge(v_lo_done, t - 1)
                sp.dma_start(v_raw[:, p, :], peer_v[0, bass.ds(t * P, P), :]).then_inc(v_loaded[p], 16)

            def store_h(t, p):
                sp.wait_ge(gelu_done, t + 1)
                sp.dma_start(h_spill[bass.ds(t, 1), :, :].rearrange("a p c -> (a p) c"), h_out[:, p, :])\
                  .then_inc(h_stored[p], 16)

            def load_h(t, p, held=True):
                if held:
                    sp.wait_ge(act_lo_done, t - 1)
                sp.wait_ge(h_stored[p], (t - p) * 8 + 16)
                sp.dma_start(h_in[:, p, :], h_spill[bass.ds(t, 1), :, :].rearrange("a p c -> (a p) c"))\
                  .then_inc(h_loaded[p], 16)

            sp.wait_ge(w_used, PROJ_CHUNKS + 4)
            load_u(0, 0, False)
            load_u(1, 1, False)
            load_v(0, 0, False)
            load_v(1, 1, False)
            load_u(2, 0)
            load_u(3, 1)
            store_h(0, 0)
            store_h(1, 1)
            with sp.Fori(0, (LAG - 2) // 2) as turn:
                t = turn * 2 + 4
                for p in range(2):
                    load_u(t + p, p)
                    store_h(t + (p - 2), p)
            for p in range(2):
                load_h(p, p, False)
            with sp.Fori(0, (TILES - LAG - 2) // 2) as turn:
                t = turn * 2 + (LAG + 2)
                for p in range(2):
                    load_u(t + p, p)
                    store_h(t + (p - 2), p)
                    load_h(t + (p - LAG), p)
                    load_v(t + (p - LAG), p)
            for t in range(TILES, TILES + 2):
                load_h(t - LAG, t % 2)
                load_v(t - LAG, t % 2)
                store_h(t - 2, t % 2)
            sp.wait_ge(ut_done, 2 * TILES)
            for q in (2, 3):
                sp.dma_start(u_raw[:, q - 2, :], peer_v[0, bass.ds((first_v + q) * P, P), :]).then_inc(vx_loaded[q - 2], 16)
            with sp.Fori(0, LAG // 4 - 1) as turn:
                for q in range(4):
                    t = turn * 4 + (first_v + 4 + q)
                    load_h(t - 2, q % 2)
                    sp.wait_ge(v_lo_done, t - 3)
                    sp.dma_start(v_slot(q)[0], peer_v[0, bass.ds(t * P, P), :]).then_inc(v_arrival(q, 0)[0], 16)
            for t in (TILES - 2, TILES - 1):
                load_h(t, t % 2)
            for h in range(HALVES):
                sp.wait_ge(y_ready[h], 2)
                sp.dma_start(out[0, h * P:(h + 1) * P, :], gate_m[:, 8 * h:8 * h + 8, :].rearrange("p a b -> p (a b)"))\
                  .then_inc(stored, 16)
            sp.wait_ge(stored, 16 * HALVES)

        @block.gpsimd
        def _(pool):
            pool.memset(ident[:, :], 0.0).then_inc(pool_step, 1)
            pool.wait_ge(pool_step, 1)
            pool.affine_select(out=ident[:, :], in_=ident[:, :], compare_op=ALU.not_equal, fill=1.0, base=0,
                               pattern=[[-1, P]], channel_multiplier=1).then_inc(ident_ready, 1)
            dist = bias_t[:, 0, :]
            pool.iota(dist[:, 0:P], pattern=[[1, P]], base=0, channel_multiplier=-1,
                      allow_small_or_imprecise_dtypes=True).then_inc(pool_step, 1)
            pool.iota(dist[:, P:3 * P], pattern=[[1, 2 * P]], base=-P, channel_multiplier=-1,
                      allow_small_or_imprecise_dtypes=True).then_inc(pool_step, 1)
            pool.wait_ge(pool_step, 3)
            for h in range(MOBA_HEADS - 1, -1, -1):
                if h == 0:
                    pool.wait_ge(pool_step, 3 + MOBA_HEADS - 1)
                pool.tensor_scalar(bias_t[:, h, :], dist[:, :], 2.0 ** -(h + 1), None, ALU.mult).then_inc(pool_step, 1)
            pool.wait_ge(pool_step, 3 + MOBA_HEADS)
            pool.affine_select(out=bias_t[:, :, 0:P], in_=bias_t[:, :, 0:P], compare_op=ALU.is_ge, fill=MASKED,
                               base=0, pattern=[[0, MOBA_HEADS], [-1, P]], channel_multiplier=1)\
                .then_inc(bias_ready, 1)
            pool.affine_select(out=bias_t[:, :, P:3 * P], in_=bias_t[:, :, P:3 * P], compare_op=ALU.is_ge, fill=MASKED,
                               base=P, pattern=[[0, MOBA_HEADS], [-1, 2 * P]], channel_multiplier=1)\
                .then_inc(bias_ready, 1)
            for q in range(4, 8):
                pool.wait_ge(qk_rs_ready, q // 2 - 1)
                pool.wait_ge(qkT_done, q - 1)
                normalise(pool, q)
            pool.wait_ge(feat_done, 12)
            pool.iota(iota16[:, :, :], pattern=[[1, TOPK], [0, HALVES * GROUP * TOPK]], base=0, channel_multiplier=0,
                      allow_small_or_imprecise_dtypes=True).then_inc(iota_ready, 1)
            pool.iota(key_no[:, :, :], pattern=[[1, N_KEYS], [0, TOK_STEP]], base=0, channel_multiplier=0,
                      allow_small_or_imprecise_dtypes=True).then_inc(iota_ready, 1)
            links = [0]

            def link(ins):
                links[0] += 1
                ins.then_inc(pool_link, 1)
                pool.wait_ge(pool_link, links[0])

            pool.wait_ge(iota_ready, 2)
            for q in range(PEER_HEADS // GROUP - 1):
                pool.wait_ge(places_ready, q + 1)
                resolve(pool, link, q)
                pool.sem_inc(resolved, 1)

        @block.scalar
        def _(act):
            act.wait_ge(ident_ready, 1)
            act.activation(tiny["unused"][:, :], ident[:, 0:2], ACT.Sqrt)
            for h in range(HALVES):
                act.wait_ge(x_loaded[h], 16)
                act.activation(scaled[:, h, :], x_sb[:, h, :], ACT.Square, accum_out=tiny["ssq"][:, h:h + 1])\
                   .then_inc(ssq_done, 1)
            def w_upper(j):
                act.wait_ge(w_loaded[j % W_LOADS], 16 * (j // W_LOADS + 1))
                need(act, w_used, j - W_PARTS + 1)
                act.activation(w_hi[:, j % W_PARTS, :, :].rearrange("p k n -> p (k n)"), w_raw[:, j % W_LOADS, :], ACT.Copy)\
                   .then_inc(w_hi_done, 1)

            act.wait_ge(ms_ready, 1)
            act.activation(tiny["sd"][:, :], tiny["ms"][:, :], ACT.Sqrt).then_inc(sd_ready, 1)
            def feat_upper(at, pair, bank, gain):
                act.wait_ge(feat_done, at)
                for i in range(2):
                    k = 2 * pair + i
                    ins = act.activation(xn_hi[:, k, :], ps[bank][:, i * SEQ:(i + 1) * SEQ], ACT.Copy,
                                         scale=gain(k))
                ins.then_inc(xn_hi_done, 1)

            w_upper(0)
            act.wait_ge(gainsT_done, 1)
            act.activation(gains[:, :], ps[0][:, 0:N_GAINS], ACT.Copy).then_inc(gains_ready, 1)
            act.wait_ge(gains_ready, 1)
            act.activation(gains[:, GQK:GQK + 3:2], gains[:, GQK:GQK + 3:2], ACT.Copy, scale=HEAD ** -0.5)\
               .then_inc(gains_ready, 1)
            act.activation(gains[:, GSUB:GSUB + 1], gains[:, GSUB:GSUB + 1], ACT.Copy, scale=1.0 - LAM_INIT)\
               .then_inc(gains_ready, 1)
            act.wait_ge(gains_ready, 3)
            for pair in range(4):
                feat_upper(pair + 1, pair, 4 + pair, lambda k: gains[:, G1 + k:G1 + k + 1])
            w_upper(1)

            def group_copies(w):
                for h in range(HALVES):
                    if h == 0:
                        act.wait_ge(proj_done, w + 1)
                    else:
                        act.wait_ge(w_used, 2 * w + 2)
                    if w in QK_TURN:
                        need(act, normed_ready, 2 * QK_TURN[w] + h - 1)
                        to = qk_raw[:, h, :]
                    else:
                        to = v_sb[:, 1 - w // 3, h, :]
                    act.activation(to, ps[group_bank(w, h)][:, :], ACT.Copy).then_inc(copied, 1)

            def qkT_evac(q, bank):
                b, h = QK_TENSOR[q // 2], q % 2
                act.wait_ge(qkT_done, q + 1)
                act.activation(qkT[:, b, :, h * P:(h + 1) * P], ps[bank][:, :].rearrange("p (b t) -> p b t", b=4),
                               ACT.Copy, scale=gains[:, GQK + b:GQK + b + 1]).then_inc(qkT_ready, 1)

            def skT_evac(j, bank):
                act.wait_ge(skT_done, j + 1)
                act.activation(skT[:, 4 * j:4 * j + 4, :], ps[bank][:, :].rearrange("p (a n) -> p a n", a=4), ACT.Copy)\
                   .then_inc(skT_ready, 1)

            def exponentials(n, slot, row):
                for h, lo, hi in ((0, 0, P), (1, P, 3 * P)):
                    c = h * INSTANCES + n
                    ins = act.activation(expd[:, slot, lo:hi], logits[:, row, lo:hi], ACT.Exp,
                                         bias=tiny["nmax"][:, c:c + 1], accum_out=tiny["sums"][:, c:c + 1])
                return ins

            def d_exps(i):
                for j in range(2):
                    act.wait_ge(d_nmax_ready, 2 * i + j + 1)
                    need(act, mixed_ready, i - 1)
                    exponentials(MOBA_HEADS + 2 * i + j, 2 * (i % 2) + j, j).then_inc(d_exp_done, 1)

            def d_probs_evac(i):
                act.wait_ge(d_probsT_done, i + 1)
                need(act, d_heads_done, i - 1)
                act.activation(probsT[:, i % 2, :], ps[5][:, 0:3 * P], ACT.Copy).then_inc(d_probsT_ready, 1)

            for j in range(PROJ_CHUNKS):
                w, stage = j // 2, j - 6
                turn = QK_TURN.get(w - 1) if j % 2 == 0 else None
                if 2 <= stage:
                    d_probs_evac(stage - 2)
                if j % 2 == 0 and w:
                    group_copies(w - 1)
                w_upper(j + 2)
                if j == 4:
                    qkT_evac(0, 4)
                    qkT_evac(1, 5)
                if turn is not None:
                    need(act, qk_ms_ready, turn)
                    act.wait_ge(copied, 2 * w)
                    act.activation(squares[:, :, :].rearrange("p a b -> p (a b)"), qk_raw[:, :, :].rearrange("p a b -> p (a b)"),
                                   ACT.Square).then_inc(sq_done, 1)
                if stage == 0:
                    act.wait_ge(dots_ready, 2)
                    act.activation(tiny["edots"][:, :], tiny["dots"][:, :], ACT.Exp).then_inc(edots_ready, 1)
                if 0 <= stage < DIFF_HEADS:
                    d_exps(stage)
                if j == PROJ_CHUNKS - 1:
                    skT_evac(0, 3)
                    skT_evac(1, 2)
                    act.wait_ge(d_heads_done, DIFF_HEADS)
                    act.wait_ge(qk_ms_ready, 4)
                    for h in range(HALVES):
                        act.activation(squares[:, h, :], ps[6 + h][:, :], ACT.Square).then_inc(d_sq_done, 1)
                if turn is not None:
                    cols = slice(16 * turn, 16 * turn + 16)
                    act.wait_ge(qk_ms_ready, turn + 1)
                    act.activation(tiny["qk_sd"][:, cols], tiny["qk_ms"][:, cols], ACT.Sqrt).then_inc(qk_sd_ready, 1)
                if j == PROJ_CHUNKS - 1:
                    act.wait_ge(d_ms_ready, 1)
                    act.activation(tiny["d_sd"][:, :], tiny["d_ms"][:, :], ACT.Sqrt).then_inc(d_sd_ready, 1)
                    act.wait_ge(edots_ready, 1)
                    act.activation(tiny["unused"][:, :], tiny["edots"][:, :], ACT.Exp)
                if j == 5:
                    qkT_evac(2, 4)
                    qkT_evac(3, 5)
                if j == 10:
                    qkT_evac(4, 4)
                    qkT_evac(5, 2)
            group_copies(5)
            qkT_evac(6, 4)
            qkT_evac(7, 2)
            skT_evac(2, 3)
            skT_evac(3, 5)

            def mix_upper(at, pair):
                act.wait_ge(feat_done, at)
                act.activation(xn_hi[:, 2 * pair:2 * pair + 2, :].rearrange("p k t -> p (k t)"), ps[pair][:, :], ACT.Copy,
                               scale=1.0 if pair < 2 else gains[:, GSUB:GSUB + 1]).then_inc(xn_hi_done, 1)

            mix_upper(5, 2)
            mix_upper(6, 3)

            def exps(n):
                act.wait_ge(nmax_ready, n + 1)
                need(act, probsT_done, n - 3)
                exponentials(n, n % 4, n % 2).then_inc(exp_done, 1)

            def probs_evac(m):
                act.wait_ge(probsT_done, m + 1)
                need(act, heads_done, m - 1)
                act.activation(probsT[:, m % 2, :], ps[2 + m % 2][:, 0:3 * P], ACT.Copy).then_inc(probsT_ready, 1)

            exps(0)
            for m in range(MOBA_HEADS):
                if m + 1 < MOBA_HEADS:
                    exps(m + 1)
                probs_evac(m)
                if m == 1:
                    w_upper(14)
            for pair in (0, 1):
                mix_upper(6 + pair + 1, pair)
            w_upper(15)
            act.activation(tiny["unused"][:, :], tiny["sd"][:, :], ACT.Sqrt)
            for h in range(HALVES):
                for c in range(2):
                    act.wait_ge(x2_done, 2 * h + c + 1)
                    act.activation(scaled[:, h, c * COLS:(c + 1) * COLS], ps[4 + 2 * h + c][:, :], ACT.Square,
                                   accum_out=tiny["ssq2"][:, 2 * h + c:2 * h + c + 1]).then_inc(ssq_done, 1)
                act.wait_ge(ms_ready, h + 2)
                act.activation(tiny["sd2"][:, h:h + 1], tiny["ms2"][:, h:h + 1], ACT.Sqrt).then_inc(sd_ready, 1)
            act.wait_ge(rstd2_ready, 2)
            act.activation(scaled[:, 1, COLS:D], ps[7][:, :], ACT.Copy, scale=tiny["rstd2"][:, 1:2]).then_inc(x2_scaled, 1)
            for pair in (0, 2):
                act.wait_ge(feat_done, 8 + pair + 1)
                for k in (2 * pair, 2 * pair + 1):
                    ins = act.activation(featT[:, k, :], ps[(pair + 2) % 4][:, (k % 2) * SEQ:(k % 2 + 1) * SEQ], ACT.Copy,
                                         scale=gains[:, G2 + k:G2 + k + 1])
                ins.then_inc(feat_ready[0], 1)
            for pair in range(4):
                act.wait_ge(feat_ready[pair % 2], pair // 2 + 1)
                act.activation(xn_hi[:, 2 * pair:2 * pair + 2, :], featT[:, 2 * pair:2 * pair + 2, :], ACT.Copy)\
                   .then_inc(xn_hi_done, 1)

            def scores_evac(hp):
                act.wait_ge(scores_done, hp + 1)
                act.activation(scores[:, :, hp, :], ps[hp % 2][:, 0:SEQ].rearrange("p (h n) -> p h n", h=2), ACT.Copy)\
                   .then_inc(scores_ready, 1)

            for hp in range(HP):
                act.wait_ge(query_done, hp + 1)
                if hp >= 2:
                    act.wait_ge(scores_done, hp - 1)
                act.activation(qT[:, hp % 2, :], ps[2 + hp % 2][:, 0:SEQ], ACT.Copy).then_inc(query_ready, 1)
                if hp == 0:
                    scores_evac(0)
                elif hp > 1:
                    scores_evac(hp - 1)
            scores_evac(HP - 1)
            def ut_split_half(t, p, b):
                need(act, ut_done, 2 * t + (b + 1))
                if b == 0:
                    need(act, h_done, t - 1)
                act.activation(ut_hi[:, p, 4 * b:4 * b + 4, :].rearrange("p a b -> p (a b)"), ps[b][:, :], ACT.Copy)\
                   .then_inc(ut_hi_done, 1)

            def ut_split(t, p):
                ut_split_half(t, p, 0)
                ut_split_half(t, p, 1)

            def gelu(t, p, bank):
                need(act, h_done, t + 1)
                need(act, h_stored[p], (t - p) * 8)
                act.activation(h_out[:, p, :], ps[bank][:, 0:SEQ], ACT.Gelu).then_inc(gelu_done, 1)

            def v_split(t, p):
                need(act, act_done, t + 1)
                need(act, v_used, t - 1)
                act.activation(act_hi[:, p, :], h_in[:, p, :], ACT.Copy).then_inc(act_hi_done, 1)
                need(act, v_loaded[p], (t - p) * 8 + 16)
                act.activation(v_hi[:, p, :], v_raw[:, p, :], ACT.Copy).then_inc(v_hi_done, 1)

            def ut_copy(t, p):
                for b in range(2):
                    need(act, ut_done, 2 * t + (b + 1))
                    if b == 0:
                        need(act, h_done, t - 1)
                    act.activation(ut_plain[:, p, 4 * b:4 * b + 4, :].rearrange("p a b -> p (a b)"), ps[b][:, :], ACT.Copy)\
                       .then_inc(ut_hi_done, 1)

            ut_copy(0, 0)
            for s in range(TAIL_TILES):
                t = s + 1
                if t < TAIL_TILES:
                    ut_copy(t, t % 2)
                else:
                    ut_split(t, t % 2)
                gelu(s, s % 2, tail_bank(s))
                if s == 1:
                    act.wait_ge(gexp_in, 1)
                    act.activation(gexp[:, :, :, :], gexp[:, :, :, :], ACT.Exp).then_inc(gexp_done, 1)

            def gate_evac(i, n):
                act.wait_ge(gate_done, 4 * i + (n + 1))
                act.activation(gate_m[:, bass.ds(i * 16 + 4 * n, 4), :].rearrange("p a b -> p (a b)"), ps[3][:, :],
                               ACT.Copy).then_inc(gate_ready, 1)

            def gate_step(i, p, first):
                s = i + TAIL_TILES
                ut_split_half(s + 1, 1 - p, 0)
                if not first:
                    gate_evac(i - 1, 2)
                ut_split_half(s + 1, 1 - p, 1)
                if not first:
                    gate_evac(i - 1, 3)
                gate_evac(i, 0)
                gelu(s, p, 2)
                gate_evac(i, 1)

            gate_step(0, 0, True)
            gate_step(1, 1, False)
            with act.Fori(0, GATE_TILES // 2 - 1) as turn:
                for p in range(2):
                    gate_step(turn * 2 + (2 + p), p, False)
            gate_evac(GATE_TILES - 1, 2)
            ut_split(LAG + 1, 1)
            gate_evac(GATE_TILES - 1, 3)
            gelu(LAG, 0, 2)
            v_split(0, 0)
            ut_split(LAG + 2, 0)
            v_split(1, 1)
            gelu(LAG + 1, 1, 3)
            v_split(2, 0)
            with act.Fori(0, (TILES - LAG - 4) // 2) as turn:
                for p in range(2):
                    s = turn * 2 + (LAG + 2 + p)
                    ut_split(s + 1, 1 - p)
                    v_split(s - (LAG - 1), 1 - p)
                    gelu(s, p, 2 + p)
            for s in range(TILES - 2, TILES):
                if s + 1 < TILES:
                    ut_split(s + 1, (s + 1) % 2)
                v_split(s - (LAG - 1), (s + 1) % 2)
                gelu(s, s % 2, 2 + s % 2)

            def last_v_split(q, e4):
                t = e4 * 4 + (first_v + q)
                raw, hi, _ = v_slot(q)
                act.wait_ge(*v_arrival(q, e4))
                if isinstance(e4, int):
                    act.wait_ge(v_used, t - 1)
                else:
                    act.wait_ge(v_used, t - 3)
                act.activation(hi, raw, ACT.Copy).then_inc(v_hi_done, 1)
                act.wait_ge(act_done, t + 1)
                act.wait_ge(v_used, t - 1)
                act.activation(act_hi[:, q % 2, :], h_in[:, q % 2, :], ACT.Copy).then_inc(act_hi_done, 1)

            last_v_split(1, 0)
            act.wait_ge(h_done, TILES)
            for q in (2, 3):
                last_v_split(q, 0)
            with act.Fori(0, LAG // 4 - 1) as turn:
                for q in range(4):
                    last_v_split(q, turn + 1)
            act.wait_ge(y_half_done, 1)
            for c in range(2):
                act.activation(gate_m[:, 4 * c:4 * c + 4, :].rearrange("p a b -> p (a b)"), ps[4 + c][:, :], ACT.Copy)\
                   .then_inc(y_ready[0], 1)
            act.wait_ge(v_used, TILES)
            act.activation(gate_m[:, 12:16, :].rearrange("p a b -> p (a b)"), ps[7][:, :], ACT.Copy).then_inc(y_ready[1], 1)

        @block.vector
        def _(dve):
            steps = [0]

            def mark(ins):
                steps[0] += 1
                ins.then_inc(dve_step, 1)
                return steps[0]

            def link(ins):
                dve.wait_ge(dve_step, mark(ins))

            dve.wait_ge(ssq_done, 2)
            dve.tensor_scalar(tiny["ms"][:, :], tiny["ssq"][:, :], 1.0 / D, EPS, ALU.mult, ALU.add).then_inc(ms_ready, 1)
            dve.wait_ge(sd_ready, 1)
            link(dve.reciprocal(tiny["rstd"][:, :], tiny["sd"][:, :]))
            for h in range(HALVES):
                dve.tensor_scalar(scaled[:, h, :], x_sb[:, h, :], tiny["rstd"][:, h:h + 1], None, ALU.mult)\
                   .then_inc(scaled_ready, 1)
            def w_rest(j):
                dve.wait_ge(w_hi_done, j + 1)
                dve.tensor_tensor(w_lo[:, j % W_PARTS, :, :].rearrange("p k n -> p (k n)"), w_raw[:, j % W_LOADS, :],
                                  w_hi[:, j % W_PARTS, :, :].rearrange("p k n -> p (k n)").bitcast(F32), ALU.subtract)\
                   .then_inc(w_lo_done, 1)

            def feat_rest(at, pair, bank, gain):
                dve.wait_ge(xn_hi_done, at)
                for i in range(2):
                    k = 2 * pair + i
                    src, hi = ps[bank][:, i * SEQ:(i + 1) * SEQ], xn_hi[:, k, :].bitcast(F32)
                    ins = dve.scalar_tensor_tensor(xn_lo[:, k, :], src, gain(k), hi, ALU.mult, ALU.subtract)
                ins.then_inc(xn_lo_done, 1)

            w_rest(0)
            for pair in range(4):
                feat_rest(pair + 1, pair, 4 + pair, lambda k: gains[:, G1 + k:G1 + k + 1])
            w_rest(1)
            dve.wait_ge(lam_loaded, 16)
            for i in range(2):
                dve.tensor_tensor_reduce(out=lam_prod[:, i, :], in0=lam_in[:, 2 * i * HEAD:(2 * i + 1) * HEAD],
                                         in1=lam_in[:, (2 * i + 1) * HEAD:(2 * i + 2) * HEAD], scale=1.0, scalar=0.0,
                                         op0=ALU.mult, op1=ALU.add, accum_out=tiny["dots"][:, i:i + 1])\
                   .then_inc(dots_ready, 1)

            def bias_and_max(n, bank, row):
                table = instance(n)[4]
                link(dve.tensor_tensor(logits[:, row, :], ps[bank][:, 0:3 * P], bias_t[:, table, :], ALU.add))
                for h, lo, hi in ((0, 0, P), (1, P, 3 * P)):
                    c = h * INSTANCES + n
                    ins = dve.tensor_reduce(tiny["nmax"][:, c:c + 1], logits[:, row, lo:hi], AX.X, ALU.max, negate=True)
                return ins

            def d_bias_and_max(i):
                for j in range(2):
                    dve.wait_ge(d_logits_done, 2 * i + j + 1)
                    need(dve, d_exp_done, 2 * (i - 1) + j + 1)
                    bias_and_max(MOBA_HEADS + 2 * i + j, 2 + j, j).then_inc(d_nmax_ready, 1)

            def mix_diff(i):
                n = MOBA_HEADS + 2 * i
                dve.wait_ge(d_exp_done, 2 * i + 2)
                need(dve, d_probsT_done, i - 1)
                for h in range(HALVES):
                    c = h * INSTANCES + n
                    ins = dve.reciprocal(tiny["rsum"][:, c:c + 2], tiny["sums"][:, c:c + 2])
                    at = mark(ins)
                dve.wait_ge(dve_step, at)
                for h in range(HALVES):
                    c = h * INSTANCES + n
                    at = mark(dve.tensor_scalar(tiny["rlam"][:, 2 * i + h:2 * i + h + 1], tiny["rsum"][:, c + 1:c + 2],
                                                tiny["lam"][:, 1:2], None, ALU.mult))
                dve.wait_ge(dve_step, at)
                for h, lo, hi in ((0, 0, P), (1, P, 3 * P)):
                    at = mark(dve.tensor_scalar(expd[:, (n + 1) % 4, lo:hi], expd[:, (n + 1) % 4, lo:hi],
                                                tiny["rlam"][:, 2 * i + h:2 * i + h + 1], None, ALU.mult))
                dve.wait_ge(dve_step, at)
                for h, lo, hi in ((0, 0, P), (1, P, 3 * P)):
                    c = h * INSTANCES + n
                    ins = dve.scalar_tensor_tensor(mixed[:, i % 2, lo:hi], expd[:, n % 4, lo:hi], tiny["rsum"][:, c:c + 1],
                                                   expd[:, (n + 1) % 4, lo:hi], ALU.mult, ALU.subtract)
                ins.then_inc(mixed_ready, 1)

            for j in range(PROJ_CHUNKS):
                w, stage = j // 2, j - 6
                turn = QK_TURN.get(w - 1) if j % 2 == 0 else None
                if stage == 0:
                    dve.wait_ge(edots_ready, 1)
                    link(dve.tensor_tensor(tiny["lam"][:, 0:1], tiny["edots"][:, 0:1], tiny["edots"][:, 1:2], ALU.subtract))
                    link(dve.tensor_scalar(tiny["lam"][:, 1:2], tiny["lam"][:, 0:1], LAM_INIT, None, ALU.add))
                    dve.wait_ge(bias_ready, 2)
                if 0 <= stage < DIFF_HEADS:
                    d_bias_and_max(stage)
                if turn is not None:
                    cols = slice(16 * turn, 16 * turn + 16)
                    dve.wait_ge(sq_done, turn + 1)
                    link(dve.tensor_reduce(tiny["qk_ss"][:, cols], squares[:, :, :].rearrange("p a (h d) -> p (a h) d", d=HEAD),
                                           AX.X, ALU.add))
                    dve.tensor_scalar(tiny["qk_ms"][:, cols], tiny["qk_ss"][:, cols], 1.0 / HEAD, EPS, ALU.mult, ALU.add)\
                       .then_inc(qk_ms_ready, 1)
                if j == PROJ_CHUNKS - 1:
                    for h in range(HALVES):
                        dve.wait_ge(d_sq_done, h + 1)
                        at = mark(dve.tensor_reduce(tiny["d_ss"][:, 4 * h:4 * h + 4],
                                                    squares[:, h, :].rearrange("p (h d) -> p h d", d=P), AX.X, ALU.add))
                    dve.wait_ge(dve_step, at)
                    dve.tensor_scalar(tiny["d_ms"][:, :], tiny["d_ss"][:, :], 1.0 / P, EPS, ALU.mult, ALU.add)\
                       .then_inc(d_ms_ready, 1)
                w_rest(j + 2)
                if turn is not None:
                    dve.wait_ge(qk_sd_ready, turn + 1)
                    ins = dve.reciprocal(tiny["qk_rs"][:, cols], tiny["qk_sd"][:, cols])
                    if turn < 2:
                        link(ins)
                        for q in (2 * turn, 2 * turn + 1):
                            need(dve, qkT_done, q - 1)
                            normalise(dve, q)
                    else:
                        ins.then_inc(qk_rs_ready, 1)
                if 0 <= stage < DIFF_HEADS:
                    mix_diff(stage)
                if j == PROJ_CHUNKS - 1:
                    dve.wait_ge(d_sd_ready, 1)
                    link(dve.reciprocal(tiny["d_rs"][:, :], tiny["d_sd"][:, :]))
                    for h in range(HALVES):
                        dve.tensor_tensor(scaled[:, h, COLS:D].rearrange("p (h d) -> p h d", d=P),
                                          ps[6 + h][:, :].rearrange("p (h d) -> p h d", d=P),
                                          tiny["d_rs"][:, 4 * h:4 * h + 4].unsqueeze(2).to_broadcast([P, DIFF_HEADS, P]),
                                          ALU.mult).then_inc(d_mix_ready, 1)
            def mix_rest(at, pair):
                dve.wait_ge(xn_hi_done, at)
                lo = xn_lo[:, 2 * pair:2 * pair + 2, :].rearrange("p k t -> p (k t)")
                hi = xn_hi[:, 2 * pair:2 * pair + 2, :].rearrange("p k t -> p (k t)").bitcast(F32)
                if pair < 2:
                    ins = dve.tensor_tensor(lo, ps[pair][:, :], hi, ALU.subtract)
                else:
                    ins = dve.scalar_tensor_tensor(lo, ps[pair][:, :], gains[:, GSUB:GSUB + 1], hi, ALU.mult, ALU.subtract)
                ins.then_inc(xn_lo_done, 1)

            for n in range(MOBA_HEADS):
                dve.wait_ge(logits_done, n + 1)
                need(dve, exp_done, n - 1)
                bias_and_max(n, n % 2, n % 2).then_inc(nmax_ready, 1)
                if n == 1:
                    mix_rest(5, 2)
                    mix_rest(6, 3)
                if n == 3:
                    w_rest(14)
            dve.wait_ge(exp_done, MOBA_HEADS)
            for h in range(HALVES):
                c = h * INSTANCES
                at = mark(dve.reciprocal(tiny["rsum"][:, c:c + MOBA_HEADS], tiny["sums"][:, c:c + MOBA_HEADS]))
            dve.wait_ge(dve_step, at)
            dve.wait_ge(heads_done, MOBA_HEADS)
            for h in range(HALVES):
                c = h * INSTANCES
                dve.tensor_tensor(scaled[:, h, 0:COLS].rearrange("p (h d) -> p h d", d=HEAD),
                                  ps[4 + h][:, :].rearrange("p (h d) -> p h d", d=HEAD),
                                  tiny["rsum"][:, c:c + MOBA_HEADS].unsqueeze(2).to_broadcast([P, MOBA_HEADS, HEAD]),
                                  ALU.mult).then_inc(mix_ready, 1)
            for pair in (0, 1):
                mix_rest(6 + pair + 1, pair)
            w_rest(15)
            for h in range(HALVES):
                dve.wait_ge(ssq_done, 2 + 2 * h + 2)
                link(dve.tensor_tensor(tiny["ssq2s"][:, h:h + 1], tiny["ssq2"][:, 2 * h:2 * h + 1],
                                       tiny["ssq2"][:, 2 * h + 1:2 * h + 2], ALU.add))
                dve.tensor_scalar(tiny["ms2"][:, h:h + 1], tiny["ssq2s"][:, h:h + 1], 1.0 / D, EPS, ALU.mult, ALU.add)\
                   .then_inc(ms_ready, 1)
                dve.wait_ge(sd_ready, h + 2)
                dve.reciprocal(tiny["rstd2"][:, h:h + 1], tiny["sd2"][:, h:h + 1]).then_inc(rstd2_ready, 1)
                dve.wait_ge(rstd2_ready, h + 1)
                for c in range(2 - h):
                    dve.tensor_scalar(scaled[:, h, c * COLS:(c + 1) * COLS], ps[4 + 2 * h + c][:, :],
                                      tiny["rstd2"][:, h:h + 1], None, ALU.mult).then_inc(x2_scaled, 1)
            for pair in (1, 3):
                dve.wait_ge(feat_done, 8 + pair + 1)
                for k in (2 * pair, 2 * pair + 1):
                    ins = dve.tensor_scalar(featT[:, k, :], ps[(pair + 2) % 4][:, (k % 2) * SEQ:(k % 2 + 1) * SEQ],
                                            gains[:, G2 + k:G2 + k + 1], None, ALU.mult)
                ins.then_inc(feat_ready[1], 1)
            for pair in range(4):
                dve.wait_ge(xn_hi_done, 8 + pair + 1)
                dve.tensor_tensor(xn_lo[:, 2 * pair:2 * pair + 2, :], featT[:, 2 * pair:2 * pair + 2, :],
                                  xn_hi[:, 2 * pair:2 * pair + 2, :].bitcast(F32), ALU.subtract).then_inc(xn_lo_done, 1)

            def top_keys(hp):
                dve.wait_ge(scores_ready, hp + 1)
                at = [0, 0]
                for r in range(2):
                    val = [key_val[:, h, hp, 8 * r:8 * r + 8] for h in range(HALVES)]
                    for h in range(HALVES):
                        if r:
                            dve.wait_ge(dve_step, at[h])
                        at[h] = mark(dve.max(val[h], scores[:, h, hp, :]))
                    for h in range(HALVES):
                        dve.wait_ge(dve_step, at[h])
                        last = mark(dve.max_index(key_idx[:, h, hp, 8 * r:8 * r + 8], val[h], scores[:, h, hp, :]))
                        if r == 0:
                            at[h] = mark(dve.match_replace(scores[:, h, hp, :], val[h], scores[:, h, hp, :], REMOVED))
                return at[1], last

            def top_candidates(i, values_at):
                dve.wait_ge(dve_step, values_at)
                v1, v2 = key_val[:, :, 2 * i, :], key_val[:, :, 2 * i + 1, :]
                mark(dve.tensor_tensor(cand[:, i % 2, :, 0:TOPK], v1[:, :, 0:1].to_broadcast([P, HALVES, TOPK]), v2, ALU.add))
                grid = [P, HALVES, TOPK - 1, 8]
                link(dve.tensor_tensor(cand[:, i % 2, :, TOPK:].rearrange("p h (a b) -> p h a b", b=8),
                                       v1[:, :, 1:].unsqueeze(3).to_broadcast(grid),
                                       v2[:, :, 0:8].unsqueeze(2).to_broadcast(grid), ALU.add))
                at = [0, 0]
                for r in range(2):
                    top = slice(8 * r, 8 * r + 8)
                    for h in range(HALVES):
                        if r:
                            dve.wait_ge(dve_step, at[h])
                        at[h] = mark(dve.max(best[:, h, i, top], cand[:, i % 2, h, :]))
                    for h in range(HALVES):
                        dve.wait_ge(dve_step, at[h])
                        last = mark(dve.max_index(pos[:, h, i, top], best[:, h, i, top], cand[:, i % 2, h, :]))
                        if r == 0:
                            at[h] = mark(dve.match_replace(cand[:, i % 2, h, :], best[:, h, i, top], cand[:, i % 2, h, :],
                                                           REMOVED))
                return last

            def places(q):
                heads = slice(GROUP * q, GROUP * q + GROUP)
                need(dve, resolved, q - 1)
                for a in range(2):
                    for h in range(HALVES):
                        mark(dve.tensor_copy(key_idb[:, q % 2, a, :, h, :],
                                             key_idx[:, h, 2 * GROUP * q + a:2 * GROUP * (q + 1):2, :]
                                             .rearrange("p g k -> p k g")))
                where = pos[:, :, heads, :].rearrange("p h g s -> p s h g")
                mark(dve.tensor_scalar(pos_u[:, 0, :, :, :], where, 3, None, ALU.logical_shift_right))
                link(dve.tensor_scalar(pos_u[:, 1, :, :, :], where, 7, None, ALU.bitwise_and))
                row, place = (pos_u[:, c, :, :, :].rearrange("p s h g -> p (s h g)") for c in range(2))
                a_of, b_of, add = (pos_b[:, c, :, :, :].rearrange("p s h g -> p (s h g)") for c in range(3))
                mark(dve.tensor_scalar(a_of, row, -1.0, 0.0, ALU.add, ALU.max))
                link(dve.tensor_scalar(add, row, 1.0, 8.0, ALU.is_equal, ALU.mult))
                link(dve.tensor_tensor(b_of, place, add, ALU.add))
                slots = HALVES * GROUP * TOPK
                dve.tensor_tensor(match[:, q % 2, :, :, :],
                                  pos_b[:, 0:2, :, :, :].rearrange("p a s h g -> p a (s h g)").unsqueeze(2)
                                  .to_broadcast([P, 2, TOPK, slots]),
                                  iota16[:, :, :].unsqueeze(1).to_broadcast([P, 2, TOPK, slots]), ALU.is_equal)\
                   .then_inc(places_ready, 1)
                dve.wait_ge(places_ready, q + 1)

            dve.wait_ge(iota_ready, 2)
            for hp in range(HP):
                values_at, last = top_keys(hp)
                if hp % 2:
                    last = top_candidates(hp // 2, values_at)
                if hp % (2 * GROUP) == 2 * GROUP - 1:
                    dve.wait_ge(dve_step, last)
                    places(hp // (2 * GROUP))
            wide = [P, HALVES, PEER_HEADS, TOPK]
            dve.tensor_tensor(gexp[:, :, :, :], best[:, :, :, :], best[:, :, :, 0:1].to_broadcast(wide), ALU.subtract)\
               .then_inc(gexp_in, 1)
            resolve(dve, link, PEER_HEADS // GROUP - 1)
            dve.wait_ge(gexp_done, 1)
            link(dve.tensor_reduce(gsum[:, 0, :, :], gexp[:, :, :, :], AX.X, ALU.add))
            link(dve.reciprocal(gsum[:, 1, :, :], gsum[:, 0, :, :]))
            for h in range(HALVES):
                dve.tensor_tensor(chosen[:, h, 2, :].rearrange("p (h k) -> p h k", k=TOPK), gexp[:, h, :, :],
                                  gsum[:, 1, h, :].unsqueeze(2).to_broadcast([P, PEER_HEADS, TOPK]), ALU.mult)\
                   .then_inc(chosen_ready, 1)

            def ut_rest_half(t, p, b):
                need(dve, ut_hi_done, 2 * t + (b + 1))
                if b == 0:
                    need(dve, h_done, t - 1)
                dve.tensor_tensor(ut_lo[:, p, 4 * b:4 * b + 4, :].rearrange("p a b -> p (a b)"), ps[b][:, :],
                                  ut_hi[:, p, 4 * b:4 * b + 4, :].rearrange("p a b -> p (a b)").bitcast(F32),
                                  ALU.subtract).then_inc(ut_lo_done, 1)

            def ut_rest(t, p):
                ut_rest_half(t, p, 0)
                ut_rest_half(t, p, 1)

            ut_rest(TAIL_TILES, TAIL_TILES % 2)
            dve.wait_ge(routesT_done, 1)
            gate_in = ps[2][:, SEQ:2 * SEQ]
            link(dve.tensor_copy(routes[:, 2, :], gate_in))
            dve.tensor_tensor(rest[:, 0, :], gate_in, routes[:, 2, :], ALU.subtract).then_inc(gates_read, 1)
            mark(dve.tensor_copy(routes[:, 0:2, :].rearrange("p a t -> p (a t)"), ps[3][:, :]))
            dve.wait_ge(gates_read, 1)
            link(dve.tensor_copy(routes[:, 3, :], rest[:, 0, :]))
            link(dve.tensor_tensor(rest[:, 1, :], rest[:, 0, :], routes[:, 3, :], ALU.subtract))
            dve.tensor_copy(routes[:, 4, :], rest[:, 1, :]).then_inc(routes_ready, 1)
            dve.wait_ge(routes_ready, 1)

            def hot_rows(i, p, b, first):
                if not first:
                    dve.wait_ge(gate_done, 4 * i + (2 * b - 2))
                cols = bass.ds(i * 16 + b * TOK_STEP, TOK_STEP)

                def rows(a, n):
                    return routes[:, a:a + n, cols].unsqueeze(2).to_broadcast([P, n, N_KEYS, TOK_STEP])

                dve.tensor_tensor(hot[:, b, :, :, :], key_no[:, :, :].unsqueeze(1).to_broadcast([P, 2, N_KEYS, TOK_STEP]),
                                  rows(0, 2), ALU.is_equal).then_inc(hot_ready, 1)
                t = i + (TAIL_TILES + 1)
                if not first:
                    ut_rest_half(t, p, b)
                elif b:
                    ut_rest_half(t, p, 0)
                dve.wait_ge(hot_ready, 4 * i + (2 * b + 1))
                dve.tensor_tensor(gated1[:, b, :, :, :],
                                  hot[:, b, 0, :, :].unsqueeze(1).to_broadcast([P, 3, N_KEYS, TOK_STEP]),
                                  rows(2, 3), ALU.mult).then_inc(hot_ready, 1)
                if first and b:
                    ut_rest_half(t, p, 1)

            def gate_step(i, p, first):
                for b in range(2):
                    hot_rows(i, 1 - p, b, first)

            gate_step(0, 0, True)
            gate_step(1, 1, False)
            with dve.Fori(0, GATE_TILES // 2 - 1) as turn:
                for p in range(2):
                    gate_step(turn * 2 + (2 + p), p, False)

            def gated(t, p):
                need(dve, h_loaded[p], (t - p) * 8 + 16)
                dve.tensor_tensor(h_in[:, p, :], h_in[:, p, :],
                                  gate_m[:, :, bass.ds(t, 1)].rearrange("p c a -> p (c a)"), ALU.mult).then_inc(act_done, 1)

            def v_rest(t, p):
                need(dve, act_hi_done, t + 1)
                need(dve, v_used, t - 1)
                dve.tensor_tensor(act_lo[:, p, :], h_in[:, p, :], act_hi[:, p, :].bitcast(F32), ALU.subtract)\
                   .then_inc(act_lo_done, 1)
                need(dve, v_hi_done, t + 1)
                dve.tensor_tensor(v_lo[:, p, :], v_raw[:, p, :], v_hi[:, p, :].bitcast(F32), ALU.subtract)\
                   .then_inc(v_lo_done, 1)

            ut_rest(LAG + 1, 1)
            dve.wait_ge(gate_ready, SEQ // 4)
            gated(0, 0)
            v_rest(0, 0)
            ut_rest(LAG + 2, 0)
            gated(1, 1)
            v_rest(1, 1)
            gated(2, 0)
            v_rest(2, 0)
            with dve.Fori(0, (TILES - LAG - 4) // 2) as turn:
                for p in range(2):
                    s = turn * 2 + (LAG + 2 + p)
                    gated(s - (LAG - 1), 1 - p)
                    ut_rest(s + 1, 1 - p)
                    v_rest(s - (LAG - 1), 1 - p)
            for s in range(TILES - 2, TILES):
                gated(s - (LAG - 1), (s + 1) % 2)
                if s + 1 < TILES:
                    ut_rest(s + 1, (s + 1) % 2)
                v_rest(s - (LAG - 1), (s + 1) % 2)

            def last_v_rest(q, e4):
                t = e4 * 4 + (first_v + q)
                raw, hi, lo = v_slot(q)
                gated(t, q % 2)
                dve.wait_ge(v_hi_done, t + 1)
                dve.tensor_tensor(lo, raw, hi.bitcast(F32), ALU.subtract).then_inc(v_lo_done, 1)
                dve.wait_ge(act_hi_done, t + 1)
                dve.tensor_tensor(act_lo[:, q % 2, :], h_in[:, q % 2, :], act_hi[:, q % 2, :].bitcast(F32), ALU.subtract)\
                   .then_inc(act_lo_done, 1)

            for q in range(1, 4):
                last_v_rest(q, 0)
            with dve.Fori(0, LAG // 4 - 1) as turn:
                for q in range(4):
                    last_v_rest(q, turn + 1)
            dve.wait_ge(v_used, TILES)
            dve.tensor_copy(gate_m[:, 8:12, :].rearrange("p a b -> p (a b)"), ps[6][:, :]).then_inc(y_ready[1], 1)

        @block.tensor
        def _(pe):
            mm = pe.matmul
            pe.wait_ge(ident_ready, 1)
            def feat_transposes(pair, bank):
                for i in range(2):
                    k = 2 * pair + i
                    for h in range(HALVES):
                        ins = pe.transpose(ps[bank][:, i * SEQ + h * P:i * SEQ + (h + 1) * P],
                                           scaled[:, h, k * P:(k + 1) * P], ident[:, :])
                ins.then_inc(feat_done, 1)

            pe.wait_ge(scaled_ready, 2)
            for pair in range(4):
                feat_transposes(pair, 4 + pair)
                if pair == 1:
                    pe.wait_ge(gains_loaded, 16 * 7)
                    pe.transpose(ps[0][:, 0:N_GAINS], gain_rows[:, :], ident[0:N_GAINS, 0:N_GAINS]).then_inc(gainsT_done, 1)

            def chunk_products(j, kh, h, bank, start, stop, ks=range(4)):
                for k in ks:
                    for n, (a, b) in enumerate(((xn_hi, w_hi), (xn_hi, w_lo), (xn_lo, w_hi))):
                        ins = mm(ps[bank][:, :], a[:, 4 * kh + k, h * P:(h + 1) * P], b[:, j % W_PARTS, k, :],
                                 start=start and k == 0 and n == 0, stop=stop and k == 3 and n == 2)
                return ins

            def qk_transposes(q, bank):
                pe.wait_ge(normed_ready, q + 1)
                for b in range(4):
                    ins = pe.transpose(ps[bank][:, b * P:(b + 1) * P], normed[:, q % 2, b * P:(b + 1) * P], ident[:, :])
                ins.then_inc(qkT_done, 1)

            def key_transposes(j, bank):
                for i in range(4):
                    ins = pe.transpose(ps[bank][:, i * P:(i + 1) * P], sk_nat[:, 4 * j + i, :], ident[:, :])
                ins.then_inc(skT_done, 1)

            def logits_of(n, bank):
                q, k, b, r, _ = instance(n)
                rows = slice(r, r + HEAD)
                mm(ps[bank][:, 0:P], qkT[rows, q, b, 0:P], qkT[rows, k, b, 0:P], start=True, stop=True)
                return mm(ps[bank][:, P:3 * P], qkT[rows, q, b, P:SEQ], qkT[rows, k, b, :], start=True, stop=True)

            def probs_transposes(src, bank):
                for i in range(3):
                    ins = pe.transpose(ps[bank][:, i * P:(i + 1) * P], src[:, i * P:(i + 1) * P], ident[:, :])
                return ins

            def times_values(pT, kind, bank, cols):
                mm(ps[bank][:, cols], pT[:, 0:P], v_sb[:, kind, 0, cols], start=True, stop=True)
                mm(ps[bank + 1][:, cols], pT[:, P:2 * P], v_sb[:, kind, 0, cols], start=True, stop=False)
                return mm(ps[bank + 1][:, cols], pT[:, 2 * P:3 * P], v_sb[:, kind, 1, cols], start=False, stop=True)

            def diff_stage(s):
                if s >= 2:
                    pe.wait_ge(mixed_ready, s - 1)
                    need(pe, d_probsT_ready, s - 2)
                    probs_transposes(mixed[:, s % 2, :], 5).then_inc(d_probsT_done, 1)
                if s < DIFF_HEADS:
                    for j in range(2):
                        need(pe, d_nmax_ready, 2 * (s - 1) + j + 1)
                        logits_of(MOBA_HEADS + 2 * s + j, 2 + j).then_inc(d_logits_done, 1)
                if s >= 2:
                    pe.wait_ge(d_probsT_ready, s - 1)
                    times_values(probsT[:, s % 2, :], 1, 6, slice((s - 2) * P, (s - 1) * P)).then_inc(d_heads_done, 1)

            for j in range(PROJ_CHUNKS):
                w, kh = divmod(j, 2)
                pe.wait_ge(w_hi_done if j < 2 else w_lo_done, j + 1)
                if j < 2:
                    for n, (a, b) in enumerate(((xn_hi, w_hi), (xn_hi, w_lo), (xn_lo, w_hi))):
                        if b is w_lo:
                            pe.wait_ge(w_lo_done, j + 1)
                        for k in range(4):
                            if k % 2 == 0:
                                pe.wait_ge(xn_lo_done if a is xn_lo else xn_hi_done, 2 * kh + k // 2 + 1)
                            for h in range(HALVES):
                                ins = mm(ps[group_bank(0, h)][:, :], a[:, 4 * kh + k, h * P:(h + 1) * P], b[:, j, k, :],
                                         start=j == 0 and n == 0 and k == 0, stop=j == 1 and n == 2 and k == 3)
                                if h == 0 and j == 1 and n == 2 and k == 3:
                                    ins.then_inc(proj_done, 1)
                    ins.then_inc(w_used, 1)
                for h in range(HALVES if j >= 2 else 0):
                    if kh == 0 and w > 1:
                        pe.wait_ge(copied, 2 * w + h - 1)
                    ins = chunk_products(j, kh, h, group_bank(w, h), kh == 0, kh == 1)
                    if h:
                        ins.then_inc(w_used, 1)
                    elif kh:
                        ins.then_inc(proj_done, 1)
                    if j == 5 and h == 0:
                        pe.wait_ge(qkT_ready, 2)
                        qk_transposes(2, 4)
                        qk_transposes(3, 5)
                if j == 3:
                    qk_transposes(0, 4)
                    qk_transposes(1, 5)
                if j == 5:
                    pe.wait_ge(qkT_ready, 4)
                if j == 6:
                    pe.wait_ge(copied, 6)
                if 5 <= j <= 10:
                    diff_stage(j - 5)
                if j == 9:
                    pe.wait_ge(d_nmax_ready, 2 * DIFF_HEADS)
                    qk_transposes(4, 4)
                    qk_transposes(5, 2)
                if j == 10:
                    pe.wait_ge(sk_loaded, 16)
                    key_transposes(0, 3)
                    pe.wait_ge(qkT_ready, 6)
                    key_transposes(1, 2)
            qk_transposes(6, 4)
            pe.wait_ge(skT_ready, 2)
            qk_transposes(7, 2)
            key_transposes(2, 3)
            pe.wait_ge(d_probsT_ready, DIFF_HEADS)
            key_transposes(3, 5)

            pe.wait_ge(qkT_ready, 8)
            pe.wait_ge(copied, 12)

            def moba_values(m):
                pe.wait_ge(probsT_ready, m + 1)
                if m == 0:
                    pe.wait_ge(skT_ready, 4)
                times_values(probsT[:, m % 2, :], 0, 4, slice(m * HEAD, (m + 1) * HEAD)).then_inc(heads_done, 1)

            def x_into(h):
                for c in range(2):
                    mm(ps[4 + 2 * h + c][:, :], ident[:, :], x_sb[:, h, c * COLS:(c + 1) * COLS], start=True, stop=False)

            def diff_out(n):
                c, k = divmod(n, 4)
                if k == 0:
                    pe.wait_ge(w_lo_done, PROJ_CHUNKS + 2 * c + 1)
                if n == 0:
                    pe.wait_ge(xn_lo_done, 6)
                chunk_products(PROJ_CHUNKS + 2 * c, 1, 1, 6 + c, False, False, [k])

            for n in range(2):
                logits_of(n, n).then_inc(logits_done, 1)
            pe.wait_ge(d_mix_ready, HALVES)
            pe.wait_ge(skT_ready, 3)
            feat_transposes(2, 2)
            feat_transposes(3, 3)
            x_into(1)
            for m in range(MOBA_HEADS):
                if m + 2 < MOBA_HEADS:
                    pe.wait_ge(nmax_ready, m + 1)
                    logits_of(m + 2, m % 2).then_inc(logits_done, 1)
                if m < 6:
                    diff_out(m)
                pe.wait_ge(exp_done, m + 1)
                need(pe, probsT_ready, m - 1)
                probs_transposes(expd[:, m % 4, :], 2 + m % 2).then_inc(probsT_done, 1)
                if m:
                    moba_values(m - 1)
            moba_values(MOBA_HEADS - 1)
            diff_out(6)
            diff_out(7)

            for h in range(HALVES):
                pe.wait_ge(mix_ready, h + 1)
                for pair in (0, 1):
                    for i in range(2):
                        k = 2 * pair + i
                        ins = pe.transpose(ps[pair][:, i * SEQ + h * P:i * SEQ + (h + 1) * P],
                                           scaled[:, h, k * P:(k + 1) * P], ident[:, :])
                    if h:
                        ins.then_inc(feat_done, 1)
            x_into(0)
            for h in range(HALVES):
                for c in range(2):
                    j = PROJ_CHUNKS + 2 * c
                    if h == 0:
                        pe.wait_ge(w_lo_done, j + 1)
                        chunk_products(j, 1, 0, 4 + c, False, False).then_inc(w_used, 1)
                        pe.wait_ge(w_lo_done, j + 2)
                        if c == 0:
                            pe.wait_ge(xn_lo_done, 8)
                    chunk_products(j + 1, 0, h, 4 + 2 * h + c, False, True).then_inc(x2_done, 1)
            pe.wait_ge(x2_done, 4)
            pe.sem_inc(w_used, 1)
            pe.sem_inc(w_used, 1)
            for h in range(HALVES):
                pe.wait_ge(x2_scaled, 2 * h + 2)
                for pair in range(4):
                    for i in range(2):
                        k = 2 * pair + i
                        ins = pe.transpose(ps[(pair + 2) % 4][:, i * SEQ + h * P:i * SEQ + (h + 1) * P],
                                           scaled[:, h, k * P:(k + 1) * P], ident[:, :])
                    if h:
                        ins.then_inc(feat_done, 1)

            def key_scores(hp):
                pe.wait_ge(query_ready, hp + 1)
                if hp >= 2:
                    pe.wait_ge(scores_ready, hp - 1)
                for h in range(HALVES):
                    ins = mm(ps[hp % 2][:, h * P:(h + 1) * P], qT[:, hp % 2, h * P:(h + 1) * P], skT[:, hp, :],
                             start=True, stop=True)
                ins.then_inc(scores_done, 1)

            for hp in range(HP):
                c = hp % 2
                j = PROJ_CHUNKS + 4 + hp // 2
                if c == 0:
                    pe.wait_ge(w_loaded[j % W_LOADS], 16 * (j // W_LOADS + 1))
                if hp >= 2:
                    pe.wait_ge(query_ready, hp - 1)
                for k in range(KD):
                    if hp == 0 and k % 2 == 0:
                        pe.wait_ge(feat_ready[k // 2 % 2], k // 4 + 1)
                    ins = mm(ps[2 + hp % 2][:, 0:SEQ], w_raw[:, j % W_LOADS, 2 * k * P + c * P:2 * k * P + (c + 1) * P],
                             featT[:, k, :], start=k == 0, stop=k == KD - 1)
                ins.then_inc(query_done, 1)
                if c == 1:
                    pe.wait_ge(query_done, hp + 1)
                    pe.sem_inc(w_used, 1)
                if hp == 0:
                    key_scores(0)
                elif hp > 1:
                    key_scores(hp - 1)
            key_scores(HP - 1)
            def transposes(t, p, halves=(0, 1), plain=False):
                if 0 in halves:
                    need(pe, u_loaded[p], (t - p) * 8 + 16)
                for b in halves:
                    if plain:
                        need(pe, ut_hi_done, 2 * t + (b - 1))
                    else:
                        need(pe, ut_lo_done, 2 * t + (b - 1 - 2 * TAIL_TILES))
                    for i in range(4):
                        k = 4 * b + i
                        ins = pe.transpose(ps[b][:, i * P:(i + 1) * P], u_raw[:, p, k * P:(k + 1) * P], ident[:, :])
                    ins.then_inc(ut_done, 1)

            def x_dot_u(t, p, bank, ks):
                for k in ks:
                    for n, (a, b) in enumerate(((ut_hi, xn_hi), (ut_hi, xn_lo), (ut_lo, xn_hi))):
                        ins = mm(ps[bank][:, 0:SEQ], a[:, p, k, :], b[:, k, :], start=k == 0 and n == 0,
                                 stop=k == KD - 1 and n == 2)
                if KD - 1 in ks:
                    ins.then_inc(h_done, 1)

            def times_v(t, p, q=None, last=False):
                need(pe, act_lo_done, t + 1)
                need(pe, v_lo_done, t + 1)
                _, hi, lo = v_slot(p if q is None else q)
                for h in range(HALVES):
                    for a, b in ((act_hi, hi), (act_hi, lo), (act_lo, hi)):
                        for c in range(2):
                            ins = mm(ps[4 + 2 * h + c][:, :], a[:, p, h * P:(h + 1) * P], b[:, c * COLS:(c + 1) * COLS],
                                     start=False, stop=True, skip_group_check=True)
                    if last and h == 0:
                        ins.then_inc(y_half_done, 1)
                ins.then_inc(v_used, 1)

            pe.wait_ge(xn_lo_done, 12)
            pe.wait_ge(scores_ready, HP)
            transposes(0, 0, plain=True)
            for s in range(TAIL_TILES):
                transposes(s + 1, (s + 1) % 2, plain=True)
                need(pe, ut_hi_done, 2 * s + 2)
                if s < TAIL_TILES - 1:
                    need(pe, gelu_done, s - 1)
                else:
                    pe.wait_ge(chosen_ready, HALVES)
                    pe.wait_ge(resolved, PEER_HEADS // GROUP - 1)
                    pe.wait_ge(gelu_done, s)
                    for h in range(HALVES):
                        for a in range(2):
                            pe.transpose(ps[3][:, a * SEQ + h * P:a * SEQ + (h + 1) * P], chosen[:, h, a, :], ident[:, :])
                        ins = pe.transpose(ps[2][:, SEQ + h * P:SEQ + (h + 1) * P], chosen[:, h, 2, :], ident[:, :])
                    ins.then_inc(routesT_done, 1)
                    pe.wait_ge(gates_read, 1)
                for k in range(KD):
                    ins = mm(ps[tail_bank(s)][:, 0:SEQ], ut_plain[:, s % 2, k, :], featT[:, k, :], start=k == 0,
                             stop=k == KD - 1)
                ins.then_inc(h_done, 1)

            def gate_tokens(i, n, first=False):
                b = n // 2
                if n % 2 == 0:
                    pe.wait_ge(hot_ready, 4 * i + (2 * b + 2))
                if not first:
                    pe.wait_ge(gate_ready, 4 * i + n)
                for j in range(4):
                    tok = 4 * (n % 2) + j
                    for a in range(3):
                        ins = mm(ps[3][:, j * P:(j + 1) * P], hot[:, b, 1, :, tok], gated1[:, b, a, :, tok],
                                 start=a == 0, stop=a == 2)
                ins.then_inc(gate_done, 1)

            def gate_step(i, p, first):
                t = i + TAIL_TILES
                pe.wait_ge(ut_lo_done, i * 2 + 1)
                need(pe, gelu_done, t)
                x_dot_u(t, p, 2, range(0, 2))
                transposes(t + 1, 1 - p, [0])
                if not first:
                    gate_tokens(i - 1, 2)
                x_dot_u(t, p, 2, range(2, 4))
                pe.wait_ge(ut_lo_done, i * 2 + 2)
                transposes(t + 1, 1 - p, [1])
                if not first:
                    gate_tokens(i - 1, 3)
                x_dot_u(t, p, 2, range(4, 6))
                gate_tokens(i, 0, first)
                x_dot_u(t, p, 2, range(6, 8))
                gate_tokens(i, 1)

            gate_step(0, 0, True)
            gate_step(1, 1, False)
            with pe.Fori(0, GATE_TILES // 2 - 1) as turn:
                for p in range(2):
                    gate_step(turn * 2 + (2 + p), p, False)

            transposes(LAG + 1, 1)
            gate_tokens(GATE_TILES - 1, 2)
            need(pe, ut_lo_done, 2 * GATE_TILES + 2)
            pe.wait_ge(gelu_done, LAG)
            x_dot_u(LAG, 0, 2, range(0, 4))
            gate_tokens(GATE_TILES - 1, 3)
            x_dot_u(LAG, 0, 2, range(4, 8))
            transposes(LAG + 2, 0)
            need(pe, ut_lo_done, 2 * GATE_TILES + 4)
            pe.wait_ge(gate_ready, SEQ // 4)
            x_dot_u(LAG + 1, 1, 3, range(KD))
            times_v(0, 0)
            times_v(1, 1)

            def full_step(s, p, last=False):
                if not last:
                    transposes(s + 1, 1 - p)
                need(pe, ut_lo_done, 2 * s + (2 - 2 * TAIL_TILES))
                need(pe, gelu_done, s - 1)
                x_dot_u(s, p, 2 + p, range(KD))
                times_v(s - LAG, p)

            with pe.Fori(0, (TILES - LAG - 4) // 2) as turn:
                for p in range(2):
                    full_step(turn * 2 + (LAG + 2 + p), p)
            full_step(TILES - 2, 0)
            full_step(TILES - 1, 1, last=True)
            with pe.Fori(0, LAG // 4 - 1) as turn:
                for q in range(4):
                    times_v(turn * 4 + (first_v + q), q % 2, q)
            for q in range(4):
                times_v(TILES - 4 + q, q % 2, q, last=q == 3)


_INS = ['x', 'norm1_g', 'w_in', 'moba_qk_norm_g', 'diff_qk_norm_g', 'diff_lambda', 'diff_subln_g', 'w_out', 'norm2_g',
        'peer_w_query', 'peer_sub_keys', 'peer_u', 'peer_v']


def kernel(**inputs):
    import numpy as _np
    import concourse.bacc as _bacc
    from concourse import mybir as _mybir
    from concourse.bass_utils import run_bass_kernel_spmd as _run

    nc = _bacc.Bacc("TRN2", target_bir_lowering=False, num_devices=1)
    arrays, args = {}, []
    for name in _INS:
        a = _np.ascontiguousarray(inputs[name])
        arrays[f"in_{name}_dram"] = a
        args.append(nc.dram_tensor(f"in_{name}_dram", a.shape, _mybir.dt.from_np(a.dtype), kind="ExternalInput").ap())
    args.append(nc.dram_tensor("out_0_dram", (1, SEQ, D), _mybir.dt.float32, kind="ExternalOutput").ap())
    layer(nc, *args)
    r = _run(nc, [arrays], core_ids=[0])
    return r.results[0]["out_0_dram"]
```
